# Optimizing a Trainium2 kernel written in Bass

```python
import math
import jax, jax.numpy as jnp
from jax import lax
import numpy as np

D_MODEL = 1024
BATCH = 1
SEQ = 1024
DEPTH = 1

HEAD_DIM = 64
N_HEADS_SB = 4
N_HEADS_DIL = 4
N_HEADS_FOX = 4
W_SB = N_HEADS_SB * HEAD_DIM
W_DIL = N_HEADS_DIL * HEAD_DIM
W_FOX = N_HEADS_FOX * HEAD_DIM
CONV_WIDTH = D_MODEL - W_SB - W_DIL - W_FOX
N_CONV_GROUPS = 4
CONV_K = 3
DIL_PATTERNS = ((128, 1), (512, 4), (2048, 16))
BLOCK_Q = 128
REL_BUCKETS = 32
REL_MAX_DIST = 2048
D_FF = ((8 * D_MODEL + 3 * 256 - 1) // (3 * 256)) * 256
PROJ_WIDTH = 3 * W_SB + 3 * W_DIL + 3 * W_FOX + 3 * CONV_WIDTH + N_HEADS_FOX
DN_ALPHA = (2 * DEPTH) ** 0.25
DN_BETA = (8 * DEPTH) ** -0.25
LN_EPS = 1e-5

kernel_name = "hybrid_parallel_sb_dilated_fox_shortconv"

def split_heads(t, n_heads):
    b, s, _ = t.shape
    return t.reshape(b, s, n_heads, HEAD_DIM).transpose(0, 2, 1, 3)

def merge_heads(t):
    b, h, s, d = t.shape
    return t.transpose(0, 2, 1, 3).reshape(b, s, h * d)

def layer_norm(x, g, b):
    xf = x.astype(jnp.float32)
    mu = jnp.mean(xf, axis=-1, keepdims=True)
    var = jnp.mean(jnp.square(xf - mu), axis=-1, keepdims=True)
    y = (xf - mu) * lax.rsqrt(var + LN_EPS) * g.astype(jnp.float32) + b.astype(jnp.float32)
    return y.astype(x.dtype)

def stick_breaking_attention(q, k, v):
    b, h, s, d = q.shape
    nb = s // BLOCK_Q
    scale = d ** -0.5
    qb = q.reshape(b, h, nb, BLOCK_Q, d).transpose(2, 0, 1, 3, 4)
    k_pos = jnp.arange(s)

    def block(args):
        q_blk, i = args
        q_pos = i * BLOCK_Q + jnp.arange(BLOCK_Q)
        z = jnp.einsum('bhqd,bhkd->bhqk', q_blk, k).astype(jnp.float32) * scale
        strict = k_pos[None, :] < q_pos[:, None]
        log_beta = jax.nn.log_sigmoid(z)
        log_rest = jnp.where(strict, jax.nn.log_sigmoid(-z), 0.0)
        tail = lax.cumsum(log_rest, axis=3, reverse=True) - log_rest
        a = jnp.where(strict, jnp.exp(log_beta + tail), 0.0)
        return jnp.einsum('bhqk,bhkd->bhqd', a.astype(v.dtype), v)

    out = lax.map(block, (qb, jnp.arange(nb)))
    return out.transpose(1, 2, 0, 3, 4).reshape(b, h, s, d)

def forgetting_attention(q, k, v, log_f):
    b, h, s, d = q.shape
    nb = s // BLOCK_Q
    scale = d ** -0.5
    cum = jnp.cumsum(log_f, axis=-1)
    qb = q.reshape(b, h, nb, BLOCK_Q, d).transpose(2, 0, 1, 3, 4)
    cb = cum.reshape(b, h, nb, BLOCK_Q).transpose(2, 0, 1, 3)
    k_pos = jnp.arange(s)

    def block(args):
        q_blk, c_blk, i = args
        q_pos = i * BLOCK_Q + jnp.arange(BLOCK_Q)
        z = (jnp.einsum('bhqd,bhkd->bhqk', q_blk, k).astype(jnp.float32) * scale
             + (c_blk[..., :, None] - cum[..., None, :]))
        z = jnp.where(k_pos[None, :] <= q_pos[:, None], z, -jnp.inf)
        p = jax.nn.softmax(z, axis=-1)
        return jnp.einsum('bhqk,bhkd->bhqd', p.astype(v.dtype), v)

    out = lax.map(block, (qb, cb, jnp.arange(nb)))
    return out.transpose(1, 2, 0, 3, 4).reshape(b, h, s, d)

def t5_bucket(dist):
    max_exact = REL_BUCKETS // 2
    nf = jnp.maximum(dist, 1).astype(jnp.float32)
    large = max_exact + (jnp.log(nf / max_exact) / math.log(REL_MAX_DIST / max_exact)
                         * (REL_BUCKETS - max_exact)).astype(jnp.int32)
    large = jnp.minimum(large, REL_BUCKETS - 1)
    return jnp.where(dist < max_exact, dist, large)

def to_residue_blocks(t, dil, n_blk):
    b, h, s, e = t.shape
    sub_len = s // dil
    t = t.reshape(b, h, sub_len, dil, e).transpose(0, 1, 3, 2, 4)
    t = jnp.pad(t, ((0, 0), (0, 0), (0, 0), (0, n_blk * BLOCK_Q - sub_len), (0, 0)))
    return t.reshape(b, h, dil, n_blk, BLOCK_Q, e)

def from_residue_blocks(t, s):
    b, h, dil, n_blk, bq, e = t.shape
    t = t.reshape(b, h, dil, n_blk * bq, e)[:, :, :, : s // dil]
    return t.transpose(0, 1, 3, 2, 4).reshape(b, h, s, e)

def with_previous_block(t):
    prev = jnp.pad(t[:, :, :, :-1], ((0, 0), (0, 0), (0, 0), (1, 0), (0, 0), (0, 0)))
    return jnp.concatenate([prev, t], axis=4)

def dilated_window_attention(q, k, v, rel_bias):
    b, h, s, d = q.shape
    scale = d ** -0.5
    outs, maxes, dens = [], [], []
    for window, dil in DIL_PATTERNS:
        n_back = window // dil
        n_blk = -(-(s // dil) // BLOCK_Q)
        qs = to_residue_blocks(q, dil, n_blk)
        kb = with_previous_block(to_residue_blocks(k, dil, n_blk))
        vb = with_previous_block(to_residue_blocks(v, dil, n_blk))
        qi = jnp.arange(BLOCK_Q)[:, None]
        kj = jnp.arange(2 * BLOCK_Q)[None, :]
        sub_dist = qi + BLOCK_Q - kj
        in_band = (sub_dist >= 0) & (sub_dist <= n_back)
        key_valid = (jnp.arange(n_blk)[:, None, None] > 0) | (kj[None] >= BLOCK_Q)
        mask = in_band[None] & key_valid
        bias = rel_bias[t5_bucket(jnp.maximum(sub_dist, 0) * dil)]
        bias = bias.transpose(2, 0, 1).astype(jnp.float32)
        z = (jnp.einsum('bhrnqd,bhrnkd->bhrnqk', qs, kb).astype(jnp.float32) * scale
             + bias[None, :, None, None])
        z = jnp.where(mask[None, None, None], z, -jnp.inf)
        m = jnp.max(z, axis=-1, keepdims=True)
        p = jnp.exp(z - m)
        den = jnp.sum(p, axis=-1, keepdims=True)
        o = jnp.einsum('bhrnqk,bhrnkd->bhrnqd', p.astype(v.dtype), vb).astype(jnp.float32) / den
        outs.append(from_residue_blocks(o, s))
        maxes.append(from_residue_blocks(m, s))
        dens.append(from_residue_blocks(den, s))
    m_all = jnp.stack(maxes)
    w = jnp.stack(dens) * jnp.exp(m_all - jnp.max(m_all, axis=0, keepdims=True))
    out = jnp.sum(w * jnp.stack(outs), axis=0) / jnp.sum(w, axis=0)
    return out.astype(q.dtype)

def short_gated_conv(b_gate, c_gate, h, conv_w):
    u = c_gate * h
    y = lax.conv_general_dilated(
        u, conv_w[:, None, :].astype(u.dtype), window_strides=(1,), padding=[(CONV_K - 1, 0)],
        dimension_numbers=('NWC', 'WIO', 'NWC'), feature_group_count=CONV_WIDTH)
    return b_gate * y

def hybrid_mixer(x, w_in, f_bias, conv_w, w_out, rel_bias):
    proj = x @ w_in
    widths = (W_SB,) * 3 + (W_DIL,) * 3 + (W_FOX,) * 3 + (CONV_WIDTH,) * 3 + (N_HEADS_FOX,)
    points, acc = [], 0
    for wdt in widths[:-1]:
        acc += wdt
        points.append(acc)
    (sb_q, sb_k, sb_v, dl_q, dl_k, dl_v, fx_q, fx_k, fx_v,
     cv_b, cv_c, cv_h, fx_f) = jnp.split(proj, points, axis=-1)
    out_a = stick_breaking_attention(split_heads(sb_q, N_HEADS_SB), split_heads(sb_k, N_HEADS_SB),
                                     split_heads(sb_v, N_HEADS_SB))
    out_b = dilated_window_attention(split_heads(dl_q, N_HEADS_DIL), split_heads(dl_k, N_HEADS_DIL),
                                     split_heads(dl_v, N_HEADS_DIL), rel_bias)
    log_f = jax.nn.log_sigmoid((fx_f + f_bias).astype(jnp.float32)).transpose(0, 2, 1)
    out_c = forgetting_attention(split_heads(fx_q, N_HEADS_FOX), split_heads(fx_k, N_HEADS_FOX),
                                 split_heads(fx_v, N_HEADS_FOX), log_f)
    out_d = short_gated_conv(cv_b, cv_c, cv_h, conv_w)
    mixed = jnp.concatenate([merge_heads(out_a), merge_heads(out_b), merge_heads(out_c),
                             out_d.astype(x.dtype)], axis=-1)
    return mixed @ w_out

def swiglu_ffn(x, w_gate, w_up, w_down):
    return (jax.nn.silu(x @ w_gate) * (x @ w_up)) @ w_down

def setup_inputs(seed: int = 0) -> dict:
    key = jax.random.key(seed)
    ks = jax.random.split(key, 13)
    f32 = jnp.float32
    nrm = lambda k, shape, s: jax.random.normal(k, shape, f32) * s
    return {
        "x": jax.random.normal(ks[0], (BATCH, SEQ, D_MODEL), f32),
        "w_in": nrm(ks[1], (DEPTH, D_MODEL, PROJ_WIDTH), D_MODEL ** -0.5),
        "f_bias": 1.0 + nrm(ks[2], (DEPTH, N_HEADS_FOX), 0.1),
        "conv_w": nrm(ks[3], (DEPTH, CONV_K, CONV_WIDTH), CONV_K ** -0.5),
        "w_out": nrm(ks[4], (DEPTH, D_MODEL, D_MODEL), D_MODEL ** -0.5 * DN_BETA),
        "rel_bias": nrm(ks[5], (REL_BUCKETS, N_HEADS_DIL), 0.1),
        "ln1_g": 1.0 + nrm(ks[6], (DEPTH, D_MODEL), 0.02),
        "ln1_b": nrm(ks[7], (DEPTH, D_MODEL), 0.02),
        "w_gate": nrm(ks[8], (DEPTH, D_MODEL, D_FF), D_MODEL ** -0.5),
        "w_up": nrm(ks[9], (DEPTH, D_MODEL, D_FF), D_MODEL ** -0.5),
        "w_down": nrm(ks[10], (DEPTH, D_FF, D_MODEL), D_FF ** -0.5 * DN_BETA),
        "ln2_g": 1.0 + nrm(ks[11], (DEPTH, D_MODEL), 0.02),
        "ln2_b": nrm(ks[12], (DEPTH, D_MODEL), 0.02),
    }

def reference(x, w_in, f_bias, conv_w, w_out, rel_bias, ln1_g, ln1_b, w_gate, w_up, w_down,
              ln2_g, ln2_b):
    for layer in range(DEPTH):
        mix = hybrid_mixer(x, w_in[layer], f_bias[layer], conv_w[layer], w_out[layer], rel_bias)
        x = layer_norm(DN_ALPHA * x + mix, ln1_g[layer], ln1_b[layer])
        ffn = swiglu_ffn(x, w_gate[layer], w_up[layer], w_down[layer])
        x = layer_norm(DN_ALPHA * x + ffn, ln2_g[layer], ln2_b[layer])
    return x


_drawn_inputs = setup_inputs


def setup_inputs(seed=0):
    import zlib

    import numpy as np

    out = dict(_drawn_inputs(seed))
    spreads = {}
    factors = {'f_bias': 53.888, 'rel_bias': 8.0, 'ln1_b': 2.751, 'ln2_g': 8.015, 'ln2_b': 8.174}
    for name, (base, spread) in spreads.items():
        noise = np.random.default_rng([zlib.crc32(name.encode()), seed]).standard_normal(out[name].shape)
        drawn = base * np.exp(spread * noise) if base else spread * noise
        out[name] = __import__('jax').numpy.asarray(drawn.astype(out[name].dtype))
    for name, factor in factors.items():
        out[name] = (out[name] * factor).astype(out[name].dtype)
    return out
```

```python
from contextlib import ExitStack

import concourse.bass as bass
import numpy as np
from concourse import mybir

F32 = mybir.dt.float32
F32R = mybir.dt.float32r
BF16 = mybir.dt.bfloat16
ACT = mybir.ActivationFunctionType
ALU = mybir.AluOpType

P = 128
S = 1024
D = 1024
KC = D // P
ST = S // P
HALF = 512
HD = 64
SCALE = HD ** -0.5
FF = 2816
FC = FF // P
GROUPS = FC // 2
GATES = 4
W_KIND = 3 * 256
CONV0 = 3 * W_KIND
GATE0 = CONV0 + 3 * 256
ALPHA = 2.0 ** 0.25
EPS = 1e-5
MASKED = 1e30
BUCKETS, MAX_DIST = 32, 2048
SB, DIL, FOX = 0, 1, 2
VW = 192
TAB = 1279
TOEP = 1152


def bucket_starts():
    d = np.arange(S)
    exact = BUCKETS // 2
    nf = np.maximum(d, 1).astype(np.float32)
    large = exact + (np.log(nf / np.float32(exact)) / np.float32(np.log(MAX_DIST / exact))
                     * np.float32(BUCKETS - exact)).astype(np.int32)
    b = np.where(d < exact, d, np.minimum(large, BUCKETS - 1))
    return [(int(k), int(np.argmax(b == k))) for k in range(BUCKETS) if (b == k).any()]


def layer(nc, x, w_in, f_bias, conv_w, w_out, rel_bias, ln1_g, ln1_b, w_gate, w_up, w_down,
          ln2_g, ln2_b, out):
    x, out = x[0], out[0]
    w_in, w_out, w_gate, w_up, w_down = w_in[0], w_out[0], w_gate[0], w_up[0], w_down[0]

    qk_scr = nc.dram_tensor("qk_scr", [6, 2, P, 2, S], F32, kind="Internal").ap()
    v_scr = nc.dram_tensor("v_scr", [6, P, 2, ST, VW], F32, kind="Internal").ap()
    tab_scr = nc.dram_tensor("tab_scr", [4, P, TAB], F32, kind="Internal").ap()
    cum_scr = nc.dram_tensor("cum_scr", [4, S], F32, kind="Internal").ap()

    X_Q = 2 * ST
    KIND_Q = 12
    PROJ_UNITS = 6 * 3
    CONV_ORDER = [("b", 0), ("c", 0), ("b", 1), ("h", 0), ("c", 1), ("h", 1)]
    CONV_COL = {"b": CONV0, "c": CONV0 + 256, "h": CONV0 + 512}
    STEPS = [(pr, h, g) for pr in range(6) for h in range(2) for g in range(4)]
    NS = len(STEPS)
    CUM = [0]
    for _, _, g in STEPS:
        CUM.append(CUM[-1] + g + 1)

    def kind(s):
        return STEPS[s][0] // 2

    def width(s):
        return (2 * STEPS[s][2] + 2) * P

    persistent, early, attn, late = ExitStack(), ExitStack(), ExitStack(), ExitStack()
    with persistent:
        def sb(stack, name, shape, dt=F32):
            return stack.enter_context(nc.sbuf_tensor(name, shape, dt))

        def sem(name):
            return persistent.enter_context(nc.semaphore(name))

        act_hi = sb(persistent, "act_hi", [P, KC, S], F32R)
        act_lo = sb(persistent, "act_lo", [P, KC, S], F32R)
        ident = sb(persistent, "ident", [P, P])
        ident_bf = sb(persistent, "ident_bf", [P, P], BF16)
        eps_t = sb(persistent, "eps_t", [P, 1])

        to_attn = ExitStack()
        conv_out = sb(to_attn, "conv_out", [P, 2, S])
        masks = sb(to_attn, "masks", [P, 2, 2, 256], BF16)
        q_st = [[sb(to_attn if par == 0 else attn, f"q_st{par}{h}", [P, S], F32R) for h in range(2)]
                for par in range(1)]
        kh_st = [[sb(to_attn, f"kh_st0{h}", [P, S], F32R) for h in range(2)]]
        kl_st = [[sb(to_attn, f"kl_st0{h}", [P, S], F32R) for h in range(2)]]
        v_t = [sb(to_attn, "v_t0", [P, 2, ST, VW], F32R)]

        raw = sb(early, "raw", [P, 3, D])
        w_hi = sb(early, "w_hi", [P, 3, D], F32R)
        w_lo = sb(early, "w_lo", [P, 3, D], F32R)
        stg = sb(early, "stg", [P, 4, 2, HALF], F32R)
        stg_v = sb(early, "stg_v", [P, 2, 2, 2, 2, VW], F32R)
        scratch = sb(early, "scratch", [P, 4, D])
        conv_u = sb(early, "conv_u", [P, S + 2])
        conv_wt = sb(early, "conv_wt", [P, 3, 2])
        rel_t = sb(early, "rel_t", [4, BUCKETS])
        fb_t = sb(early, "fb_t", [4, 1])
        x_tile = scratch
        conv_b, conv_y, conv_c = scratch[:, 0:2, :], scratch[:, 2, :], scratch[:, 3, :]
        early.close()

        for lst, nm in ((q_st, "q_st1"), (kh_st, "kh_st1"), (kl_st, "kl_st1")):
            lst.append([sb(attn, f"{nm}{h}", [P, S], F32R) for h in range(2)])
        v_t.append(sb(attn, "v_t1", [P, 2, ST, VW], F32R))
        probs = sb(attn, "probs", [P, 2, 2, S])
        rest = sb(attn, "rest", [P, 2, S])
        pt_hi = sb(attn, "pt_hi", [P, 3, 2, 256], F32R)
        pt_lo = sb(attn, "pt_lo", [P, 3, 2, 256], F32R)
        bias_t = sb(attn, "bias_t", [P, 2, TOEP])
        negmax = sb(attn, "negmax", [P, 4])
        den = sb(attn, "den", [P, 4])
        rden = sb(attn, "rden", [P, 4])
        attn.close()
        to_attn.close()

        y = sb(late, "y", [P, ST, D])
        raw3 = sb(late, "raw3", [P, 3, D])
        w3_hi = sb(late, "w3_hi", [P, 6, D], F32R)
        w3_lo = sb(late, "w3_lo", [P, 6, D], F32R)
        h_hi = sb(late, "h_hi", [P, 2, 2, S], F32R)
        h_lo = sb(late, "h_lo", [P, 2, 2, S], F32R)
        silu_t = sb(late, "silu_t", [P, 2, HALF])
        h_t = sb(late, "h_t", [P, 2, HALF])
        gb = sb(late, "gb", [P, 2, D])
        stats = sb(late, "stats", [P, 2, 2, 6])
        mv = sb(late, "mv", [P, 2, 2])
        std = sb(late, "std", [P, 2, 2])
        late.close()

        psA = persistent.enter_context(nc.psum_tensor("psA", [P, 4, HALF], F32))
        psB = persistent.enter_context(nc.psum_tensor("psB", [P, 4, HALF], F32))

        x_loaded = [sem(f"x_loaded{i}") for i in range(4)]
        small_loaded = sem("small_loaded")
        consts_ready = sem("consts_ready")
        raw_loaded = [sem(f"raw_loaded{i}") for i in range(3)]
        whi_ready, wlo_ready = sem("whi_ready"), sem("wlo_ready")
        q_done, q_hi, q_lo = sem("q_done"), sem("q_hi"), sem("q_lo")
        stored_qk = [sem(f"stored_qk{i}") for i in range(4)]
        stored_v = [sem(f"stored_v{i}") for i in range(2)]
        gap_zeroed = sem("gap_zeroed")
        tab_ready, tab_stored = sem("tab_ready"), sem("tab_stored")
        conv_done, conv_act, conv_dve = sem("conv_done"), sem("conv_act"), sem("conv_dve")
        conv_ready = sem("conv_ready")
        gate_step = sem("gate_step")
        cum_ready, cum_stored = sem("cum_ready"), sem("cum_stored")
        qkv_loaded = [sem("qkv_loaded0"), sem("qkv_loaded1")]
        bias_loaded = [sem("bias_loaded0"), sem("bias_loaded1")]
        z_ready, z_read_act, z_read_dve = sem("z_ready"), sem("z_read_act"), sem("z_read_dve")
        exp_done, rden_ready, probs_ready = sem("exp_done"), sem("rden_ready"), sem("probs_ready")
        rest_scanned = sem("rest_scanned")
        pt_ready, pt_hi_done, pt_lo_done = sem("pt_ready"), sem("pt_hi_done"), sem("pt_lo_done")
        pv_done, o_hi, o_lo = sem("pv_done"), sem("o_hi"), sem("o_lo")
        conv_split = sem("conv_split")
        raw3_loaded = [sem(f"raw3_loaded{i}") for i in range(3)]
        w3hi_ready, w3lo_ready = sem("w3hi_ready"), sem("w3lo_ready")
        res_loaded, ln_rows = [sem(f"res_loaded{i}") for i in range(ST)], sem("ln_rows")
        wo_done, y_added = sem("wo_done"), sem("y_added")
        ln_stats, ln_std, ln_step, ln_done = sem("ln_stats"), sem("ln_std"), sem("ln_step"), sem("ln_done")
        x1_t, x1_hi, x1_scaled = sem("x1_t"), sem("x1_hi"), sem("x1_scaled")
        gu_done, silu_done, h_done = sem("gu_done"), sem("silu_done"), sem("h_done")
        hhi_done, hlo_done = sem("hhi_done"), sem("hlo_done")
        dn_done, psb_drained = sem("dn_done"), sem("psb_drained")
        stored = sem("stored")
        dve_step = sem("dve_step")

        def in_unit(col):
            return w_in[:, col].rearrange("(k p) n -> p k n", p=P)

        def as_chunks(slot):
            return slot.rearrange("p (k n) -> p k n", k=KC)

        block = persistent.enter_context(nc.Block())

        @block.sync
        def _(sp):
            for st in range(4):
                sp.dma_start(x_tile[:, st, :], x[st * P:(st + 1) * P, :]).then_inc(x_loaded[st], 16)
            sp.dma_start(rel_t[:, :], rel_bias.rearrange("b h -> h b"), allow_slow_non_contiguous=True).then_inc(small_loaded, 16)
            sp.dma_start(fb_t[:, :], f_bias.rearrange("a h -> h a"), allow_slow_non_contiguous=True).then_inc(small_loaded, 16)
            sp.dma_start(conv_wt[:, :, :], conv_w[0].rearrange("j (c p) -> p j c", p=P),
                         allow_slow_non_contiguous=True)\
              .then_inc(small_loaded, 16)

            QK_COL = [0, 256, 128, 384]

            def load_qk(col, slot):
                sp.dma_start(as_chunks(raw[:, slot, :]), in_unit(col)).then_inc(raw_loaded[slot], 16)

            def load_v(kind_i, half, slot):
                rows = w_in[half * HALF:(half + 1) * HALF, bass.ds(kind_i * W_KIND + 512, 256)]
                sp.dma_start(raw[:, slot, :].rearrange("p (k n) -> p k n", k=4),
                             rows.rearrange("(k p) n -> p k n", p=P)).then_inc(raw_loaded[slot], 16)

            for c in range(3):
                load_qk(slice(QK_COL[c], QK_COL[c] + P), c)
            for st in range(4, ST):
                sp.wait_ge(q_done, 2 * (st - 3))
                sp.dma_start(x_tile[:, st % 4, :], x[st * P:(st + 1) * P, :])\
                  .then_inc(x_loaded[st % 4], 16)
            sp.wait_ge(tab_ready, 1)
            tab_row = conv_out[0:4].rearrange("p a n -> p (a n)")[:, 0:TAB]
            sp.dma_start(tab_scr, tab_row.unsqueeze(1).broadcast_to([4, P, TAB])).then_inc(tab_stored, 16)

            with sp.Fori(0, 3) as i:
                for c in range(6):
                    sp.wait_ge(whi_ready, 6 * i + (c + 1))
                    sp.wait_ge(wlo_ready, 6 * i + (c + 1))
                    if c == 0:
                        load_qk(bass.ds(i * W_KIND + QK_COL[3], P), 0)
                    elif c < 3:
                        load_v(i, c - 1, c)
                    else:
                        load_qk(bass.ds(i * W_KIND + (W_KIND + QK_COL[c - 3]), P), c - 3)
                    if c < 4:
                        for n in range(2):
                            sp.wait_ge(q_lo, 12 * i + (X_Q + 2 * c + n + 1))
                            slot = (2 * c + n) % 4
                            sp.dma_start(
                                qk_scr[bass.ds(2 * i + c // 2, 1), c % 2, :, :, n * HALF:(n + 1) * HALF]
                                .rearrange("a p t n -> (a p) t n"),
                                stg[:, slot, :, :].bitcast(F32)).then_inc(stored_qk[slot], 16)
                    elif c == 5:
                        for v in range(4):
                            sp.wait_ge(q_lo, 12 * i + (X_Q + 8 + v + 1))
                            for pr in range(2):
                                sp.dma_start(
                                    v_scr[bass.ds(2 * i + pr, 1), :, :, 2 * v:2 * v + 2, :]
                                    .rearrange("a p t s n -> (a p) t (s n)"),
                                    stg_v[:, v % 2, :, pr, :, :].rearrange("p t s n -> p t (s n)").bitcast(F32))\
                                  .then_inc(stored_v[v % 2], 16)
            for c in range(3, 7):
                u = PROJ_UNITS + c
                sp.wait_ge(whi_ready, u - 2)
                sp.wait_ge(wlo_ready, u - 2)
                if c < 6:
                    what, ch = CONV_ORDER[c]
                    col = CONV_COL[what] + ch * P
                    load_qk(slice(col, col + P), u % 3)
                else:
                    dst = as_chunks(raw[:, u % 3, :])
                    sp.dma_start(dst[:, :, 0:GATES], in_unit(slice(GATE0, GATE0 + GATES)))\
                      .then_inc(raw_loaded[u % 3], 16)
                    sp.dma_start(dst[:, :, GATES:P], in_unit(slice(0, P - GATES)))\
                      .then_inc(raw_loaded[u % 3], 16)

            for k in range(4):
                sp.wait_ge(stored_qk[k], 16 * 6)
            for k in range(2):
                sp.wait_ge(stored_v[k], 16 * 12)

            def load_pair(pr):
                par = pr % 2
                for h in range(2):
                    for which, part, stride, dst in ((0, 0, S, q_st), (1, 0, 0, kh_st), (1, 1, 0, kl_st)):
                        at = ((pr * 2 + which) * P + h * HD) * 2 * S + part * S
                        sp.dma_start(dst[par][h][:, :].bitcast(F32),
                                     bass.AP(qk_scr.tensor, at, [[stride, 2], [2 * S, HD], [1, S]]))\
                          .then_inc(qkv_loaded[par], 16)
                sp.dma_start(v_t[par][:, :, :, :].bitcast(F32), v_scr[pr]).then_inc(qkv_loaded[par], 16)

            def load_bias(hd):
                if hd < 8:
                    src = bass.AP(tab_scr.tensor, (hd - 4) * P * TAB + P - 1, [[TAB - 1, P], [1, TOEP]])
                    dst = bias_t[:, hd % 2, :]
                else:
                    src = bass.AP(cum_scr.tensor, (hd - 8) * S, [[0, P], [1, S]])
                    dst = bias_t[:, hd % 2, 0:S]
                sp.dma_start(dst, src).then_inc(bias_loaded[hd % 2], 16)

            load_pair(0)
            sp.wait_ge(tab_stored, 16)
            sp.wait_ge(cum_ready, 1)
            sp.dma_start(cum_scr, conv_u[0:4, 0:S]).then_inc(cum_stored, 16)
            sp.wait_ge(cum_stored, 16)
            sp.wait_ge(conv_ready, 2)
            load_pair(1)
            load_bias(4)
            load_bias(5)
            for pr in range(2, 6):
                sp.wait_ge(pv_done, CUM[8 * (pr - 1)])
                load_pair(pr)
                for hd in (2 * pr + 2, 2 * pr + 3) if pr >= 2 else ():
                    if hd < 12:
                        sp.wait_ge(z_read_dve, 8 * (hd - 2 - 4) + 8)
                        load_bias(hd)

            sp.wait_ge(pv_done, CUM[NS])
            sp.wait_ge(o_lo, NS)
            sp.wait_ge(conv_split, 2)

            def slot_free(u):
                if isinstance(u, int) and u < 3:
                    return
                sp.wait_ge(w3hi_ready, u - 2)
                sp.wait_ge(w3lo_ready, u - 2)

            for u in range(8):
                slot_free(u)
                nh, kp = divmod(u, 4)
                src = w_out[2 * kp * P:(2 * kp + 2) * P, nh * HALF:(nh + 1) * HALF]
                sp.dma_start(raw3[:, u % 3, :].rearrange("p (k n) -> p k n", k=2),
                             src.rearrange("(k p) n -> p k n", p=P)).then_inc(raw3_loaded[u % 3], 16)
                if u == 2:
                    for st in range(ST):
                        sp.dma_start(y[:, st, :], x[st * P:(st + 1) * P, :])\
                          .then_inc(res_loaded[st], 16)
                    for k, row in enumerate((ln1_g, ln1_b)):
                        sp.dma_start(gb[:, k, :], bass.AP(row.tensor, 0, [[0, P], [1, D]]))\
                          .then_inc(ln_rows, 16)

            def load_gu(u, slot, w, chunk):
                slot_free(u)
                sp.dma_start(as_chunks(raw3[:, slot, :]),
                             w[:, bass.ds(chunk * P, P)].rearrange("(k p) n -> p k n", p=P))\
                  .then_inc(raw3_loaded[slot], 16)

            def load_dn(u, slot, chunk):
                slot_free(u)
                sp.dma_start(raw3[:, slot, :], w_down[bass.ds(chunk * P, P), :])\
                  .then_inc(raw3_loaded[slot], 16)

            for c in range(2):
                load_gu(8 + 2 * c, (8 + 2 * c) % 3, w_gate, c)
                load_gu(9 + 2 * c, (9 + 2 * c) % 3, w_up, c)
            with sp.Fori(0, (GROUPS - 1) // 2) as it:
                for j in range(2):
                    at = 12 + 6 * j
                    load_gu(12 * it + at, at % 3, w_gate, 4 * it + (2 * j + 2))
                    load_gu(12 * it + (at + 1), (at + 1) % 3, w_up, 4 * it + (2 * j + 2))
                    load_dn(12 * it + (at + 2), (at + 2) % 3, 4 * it + 2 * j)
                    load_dn(12 * it + (at + 3), (at + 3) % 3, 4 * it + (2 * j + 1))
                    load_gu(12 * it + (at + 4), (at + 4) % 3, w_gate, 4 * it + (2 * j + 3))
                    load_gu(12 * it + (at + 5), (at + 5) % 3, w_up, 4 * it + (2 * j + 3))
            load_dn(72, 0, FC - 2)
            load_dn(73, 1, FC - 1)
            sp.wait_ge(ln_done, ST)
            for k, row in enumerate((ln2_g, ln2_b)):
                sp.dma_start(gb[:, k, :], bass.AP(row.tensor, 0, [[0, P], [1, D]]))\
                  .then_inc(ln_rows, 16)
            for st in range(ST):
                sp.wait_ge(ln_done, ST + st + 1)
                sp.dma_start(out[st * P:(st + 1) * P, :], y[:, st, :]).then_inc(stored, 16)
            sp.wait_ge(stored, 16 * ST)

        @block.gpsimd
        def _(pool):
            pool.memset(ident[:, :], 0.0).then_inc(consts_ready, 1)
            pool.wait_ge(consts_ready, 1)
            pool.affine_select(out=ident[:, :], in_=ident[:, :], compare_op=ALU.not_equal, fill=1.0,
                               base=0, pattern=[[-1, P]], channel_multiplier=1).then_inc(consts_ready, 1)
            pool.memset(stg_v[:, :, :, :, :, HD:P].rearrange("p s t r k n -> p (s t r k) n").bitcast(F32),
                        0.0).then_inc(gap_zeroed, 1)
            pool.memset(conv_u[:, 0:2], 0.0).then_inc(gap_zeroed, 1)
            pool.memset(eps_t[:, :], EPS).then_inc(gap_zeroed, 1)
            pool.wait_ge(consts_ready, 2)
            pool.tensor_copy(ident_bf[:, :], ident[:, :]).then_inc(consts_ready, 1)
            pool.memset(masks[:, :, :, :].rearrange("p a b n -> p (a b n)"), 0.0).then_inc(consts_ready, 1)
            pool.wait_ge(consts_ready, 4)
            for strict in range(2):
                for a in range(2):
                    m = masks[:, strict, a, :]
                    pool.affine_select(out=m, in_=m, compare_op=ALU.is_gt if strict else ALU.is_ge,
                                       fill=MASKED, base=a * P, pattern=[[-1, 256]],
                                       channel_multiplier=1).then_inc(consts_ready, 1)

            def split_lo(u, slot, n_loaded):
                pool.wait_ge(raw_loaded[slot], n_loaded)
                pool.wait_ge(whi_ready, u + 1)
                pool.tensor_tensor(w_lo[:, slot, :], raw[:, slot, :], w_hi[:, slot, :].bitcast(F32),
                                   ALU.subtract).then_inc(wlo_ready, 1)

            with pool.Fori(0, 3) as i:
                for c in range(6):
                    split_lo(6 * i + c, c % 3, 32 * i + 16 * (c // 3 + 1))
            for c in range(7):
                u = PROJ_UNITS + c
                split_lo(u, u % 3, 16 * (u // 3 + 1) + 16 * (c == 6))

            for ch in range(2):
                pool.wait_ge(q_hi, X_Q + 3 * KIND_Q + ch + 1)
                pool.tensor_tensor(act_lo[:, 6 + ch, :], conv_out[:, ch, :],
                                   act_hi[:, 6 + ch, :].bitcast(F32), ALU.subtract).then_inc(conv_split, 1)

            def split3_lo(u, slot, n_loaded):
                pool.wait_ge(raw3_loaded[slot % 3], n_loaded)
                pool.wait_ge(w3hi_ready, u + 1)
                pool.tensor_tensor(w3_lo[:, slot, :], raw3[:, slot % 3, :], w3_hi[:, slot, :].bitcast(F32),
                                   ALU.subtract).then_inc(w3lo_ready, 1)

            for u in range(12):
                split3_lo(u, u % 6, 16 * (u // 3 + 1))
            with pool.Fori(0, (GROUPS - 1) // 2) as it:
                for c in range(12):
                    split3_lo(12 * it + (12 + c), c % 6, 64 * it + 16 * (4 + c // 3 + 1))
            for u in (72, 73):
                split3_lo(u, u % 6, 16 * (u // 3 + 1))

        @block.scalar
        def _(act):
            def split_hi(slot, n_loaded):
                act.wait_ge(raw_loaded[slot], n_loaded)
                act.activation(w_hi[:, slot, :], raw[:, slot, :], ACT.Copy).then_inc(whi_ready, 1)

            for c in range(3):
                split_hi(c, 16)
            for Q in range(X_Q):
                st, h = divmod(Q, 2)
                act.wait_ge(q_done, Q + 1)
                act.activation(act_hi[:, 4 * h:4 * h + 4, st * P:(st + 1) * P],
                               psA[:, Q % 4, :].rearrange("p (k n) -> p k n", k=4), ACT.Copy)\
                   .then_inc(q_hi, 1)

            act.wait_ge(gap_zeroed, 1)
            with act.Fori(0, 3) as i:
                for c in range(6):
                    if c < 4:
                        for n in range(2):
                            Q = 2 * c + n
                            act.wait_ge(q_done, 12 * i + (X_Q + Q + 1))
                            if Q >= 4:
                                act.wait_ge(stored_qk[Q % 4], 32 * i + 16)
                            act.activation(stg[:, Q % 4, 0, :], psA[:, Q % 4, :], ACT.Copy,
                                           scale=-SCALE if c % 2 == 0 else 1.0).then_inc(q_hi, 1)
                    elif c == 5:
                        for v in range(4):
                            act.wait_ge(q_done, 12 * i + (X_Q + 8 + v + 1))
                            if v >= 2:
                                act.wait_ge(stored_v[v % 2], 64 * i + 32)
                            for pr in range(2):
                                op = act.activation(
                                    stg_v[:, v % 2, 0, pr, :, :]
                                    .rearrange("p s (w n) -> p s w n", n=HD)[:, :, 0:3:2, :],
                                    psA[:, v, :].rearrange("p (s r w n) -> p s r w n", s=2, r=2, w=2)
                                    [:, :, pr, :, :], ACT.Copy)
                            op.then_inc(q_hi, 1)
                    for d in {4: (), 5: (4, 5)}.get(c, (c,)):
                        split_hi(d % 3, 32 * i + 16 * ((d + 3) // 3 + 1))
                for k in range(4):
                    act.wait_ge(stored_qk[k], 32 * i + 32)
                for k in range(2):
                    act.wait_ge(stored_v[k], 64 * i + 64)

            split_next = [PROJ_UNITS + 3]

            def next_unit():
                u = split_next[0]
                if u <= PROJ_UNITS + 6:
                    split_next[0] += 1
                    act.wait_ge(conv_done, 2 * (u - 2 - PROJ_UNITS))
                    split_hi(u % 3, 16 * (u // 3 + 1) + 16 * (u == PROJ_UNITS + 6))

            act.wait_ge(tab_ready, 1)
            for c, (what, ch) in enumerate(CONV_ORDER):
                for n in range(2):
                    if what == "h":
                        continue
                    act.wait_ge(conv_done, 2 * c + n + 1)
                    if (what, ch, n) == ("c", 1, 0):
                        act.wait_ge(conv_dve, 2)
                    dst = conv_b[:, ch, n * HALF:(n + 1) * HALF] if what == "b" else \
                        conv_c[:, n * HALF:(n + 1) * HALF]
                    act.activation(dst, psB[:, (2 * c + n) % 4, :], ACT.Copy).then_inc(conv_act, 1)
                next_unit()
            gate_f = conv_c[0:GATES, :]
            gate_e = conv_b[0:GATES, 0, :]
            act.wait_ge(conv_dve, 4)
            act.wait_ge(conv_ready, 2)
            for n in range(2):
                act.wait_ge(conv_done, 13 + n)
                act.activation(gate_f[:, n * HALF:(n + 1) * HALF], psB[0:GATES, n, :], ACT.Identity,
                               bias=fb_t[:, 0:1]).then_inc(gate_step, 1)
            act.wait_ge(gate_step, 2)
            act.activation(gate_e, gate_f, ACT.Abs).then_inc(gate_step, 1)
            act.wait_ge(gate_step, 3)
            act.activation(gate_e, gate_e, ACT.Exp, scale=-1.0).then_inc(gate_step, 1)
            act.wait_ge(gate_step, 4)
            act.activation(gate_e, gate_e, ACT.Ln, bias=1.0).then_inc(gate_step, 1)

            for ch in range(2):
                act.activation(act_hi[:, 6 + ch, :], conv_out[:, ch, :], ACT.Copy).then_inc(q_hi, 1)

            def softmax_part(s, a):
                t, par, W = 2 * s + a, s % 2, width(s)
                if s >= 2:
                    act.wait_ge(pt_ready, CUM[s - 1])
                if kind(s) == SB:
                    z = psA[:, 2 * a:2 * a + 2, :].rearrange("p b n -> p (b n)")[:, 0:W]
                    if s == 0 and a == 0:
                        act.wait_ge(cum_stored, 16)
                        act.wait_ge(conv_ready, 2)
                    act.wait_ge(z_ready, t + 1)
                    act.activation(probs[:, par, a, 0:W], z, ACT.Sigmoid, scale=-1.0)
                    if s >= 1:
                        act.wait_ge(probs_ready, t - 1)
                    act.activation(rest[:, a, 0:W], z, ACT.Sigmoid).then_inc(z_read_act, 1)
                else:
                    act.wait_ge(z_read_dve, t - 32 + 1)
                    act.activation(probs[:, par, a, 0:W], probs[:, par, a, 0:W], ACT.Exp,
                                   bias=negmax[:, t % 4:t % 4 + 1], scale=-1.0,
                                   accum_out=den[:, t % 4:t % 4 + 1]).then_inc(exp_done, 1)

            def transposed_hi(s, j):
                k = CUM[s] + j
                act.wait_ge(pt_ready, k + 1)
                if k >= 3:
                    act.wait_ge(pv_done, k - 2)
                act.activation(pt_hi[:, k % 3, :, :].rearrange("p b n -> p (b n)"), psB[:, k % 2, :],
                               ACT.Copy).then_inc(pt_hi_done, 1)

            def mixed_hi(s):
                pr, h, g = STEPS[s]
                act.wait_ge(pv_done, CUM[s + 1])
                lanes = slice(h * HD, (h + 1) * HD)
                act.activation(act_hi[lanes, pr, g * 256:(g + 1) * 256], psB[lanes, 2 + s % 2, 0:256],
                               ACT.Copy).then_inc(o_hi, 1)

            softmax_part(0, 0)
            softmax_part(0, 1)
            for s in range(NS):
                g = STEPS[s][2]
                transposed_hi(s, 0)
                if s >= 1:
                    mixed_hi(s - 1)
                if s + 1 < NS:
                    softmax_part(s + 1, 0)
                if g >= 1:
                    transposed_hi(s, 1)
                if s + 1 < NS:
                    softmax_part(s + 1, 1)
                for j in range(2, g + 1):
                    transposed_hi(s, j)
            mixed_hi(NS - 1)

            def split3_hi(slot, n_loaded):
                act.wait_ge(raw3_loaded[slot % 3], n_loaded)
                act.activation(w3_hi[:, slot, :], raw3[:, slot % 3, :], ACT.Copy).then_inc(w3hi_ready, 1)

            def split3(u):
                if u >= 6:
                    act.wait_ge(wo_done, ST if u < 10 else 2 * ST)
                split3_hi(u % 6, 16 * (u // 3 + 1))

            def ln_root(n, st):
                act.wait_ge(ln_stats, n + 1)
                act.activation(std[:, st % 2, 0:1], mv[:, st % 2, 1:2], ACT.Sqrt, bias=eps_t[:, 0:1])\
                   .then_inc(ln_std, 1)

            def x1_hi_part(st):
                for h in range(2):
                    q = 2 * st + h
                    act.wait_ge(x1_t, q + 1)
                    act.activation(act_hi[:, 4 * h:4 * h + 4, st * P:(st + 1) * P],
                                   psB[:, q % 4, :].rearrange("p (k n) -> p k n", k=4), ACT.Copy)\
                       .then_inc(x1_hi, 1)
                act.activation(y[:, st, :], y[:, st, :], ACT.Copy, scale=ALPHA).then_inc(x1_scaled, 1)

            for u in range(10):
                split3(u)
            for st in range(ST + 2):
                if st < ST:
                    ln_root(st, st)
                if st >= 2:
                    x1_hi_part(st - 2)
            for u in range(10, 14):
                split3(u)

            def gated_unit(n_gu, buf, par, ch):
                for n in range(2):
                    act.wait_ge(gu_done, n_gu + n + 1)
                    act.activation(silu_t[:, n, :], psA[:, 2 * n, :], ACT.Silu).then_inc(silu_done, 1)
                for n in range(2):
                    act.wait_ge(h_done, n_gu + n + 1)
                    act.activation(h_hi[:, par, ch, n * HALF:(n + 1) * HALF], h_t[:, n, :], ACT.Copy)\
                       .then_inc(hhi_done, 1)

            gated_unit(0, None, 0, 0)
            gated_unit(2, None, 0, 1)
            with act.Fori(0, (GROUPS - 1) // 2) as it:
                for j in range(2):
                    for m in range(3):
                        for c in range(2):
                            u = 12 + 6 * j + 2 * m + 2 + c
                            split3_hi(u % 6, 64 * it + 16 * (u // 3 + 1))
                        if m != 1:
                            gated_unit(8 * it + (4 + 4 * j + m), None, (j + 1) % 2, m // 2)
            for st in range(ST):
                ln_root(ST + st, st)

        @block.vector
        def _(dve):
            chained = [0]

            def chain(op):
                chained[0] += 1
                op.then_inc(dve_step, 1)
                dve.wait_ge(dve_step, chained[0])

            for Q in range(X_Q):
                st, h = divmod(Q, 2)
                part = (slice(None), slice(4 * h, 4 * h + 4), slice(st * P, (st + 1) * P))
                dve.wait_ge(q_hi, Q + 1)
                dve.tensor_tensor(act_lo[part], psA[:, Q % 4, :].rearrange("p (k n) -> p k n", k=4),
                                  act_hi[part].bitcast(F32), ALU.subtract).then_inc(q_lo, 1)

            tab = conv_out[0:4].rearrange("p a n -> p (a n)")[:, 0:TAB]
            base = conv_u[0:4, 2:2 + S]
            dve.wait_ge(small_loaded, 48)
            chain(dve.memset(base, 0.0))
            chain(dve.memset(tab, MASKED))
            starts = bucket_starts()
            for n, (b, d0) in enumerate(starts):
                d1 = starts[n + 1][1] if n + 1 < len(starts) else S
                seg = base[:, S - d1:S - d0]
                op = dve.scalar_tensor_tensor(out=seg, in0=seg, scalar=rel_t[:, b:b + 1], in1=seg,
                                              op0=ALU.subtract, op1=ALU.add)
            chain(op)
            for lo, hi, step, count in ((0, 128, 1, 1), (0, 128, 4, 2), (0, 128, 16, 3),
                                        (132, 512, 4, 1), (144, 512, 16, 2), (528, 1008, 16, 1)):
                sel = slice(S - 1 - hi, S - lo, step)
                chain(dve.tensor_scalar(tab[:, sel], base[:, sel], -float(np.log(count)), None, ALU.add))
            dve.memset(base, 0.0).then_inc(tab_ready, 1)

            dve.wait_ge(gap_zeroed, 1)
            with dve.Fori(0, 3) as i:
                for c in range(4):
                    for n in range(2):
                        Q = 2 * c + n
                        dve.wait_ge(q_hi, 12 * i + (X_Q + Q + 1))
                        if c % 2 == 0:
                            op = dve.scalar_tensor_tensor(
                                out=stg[:, Q % 4, 1, :], in0=psA[:, Q % 4, :], scalar=-SCALE,
                                in1=stg[:, Q % 4, 0, :].bitcast(F32), op0=ALU.mult, op1=ALU.subtract)
                        else:
                            op = dve.tensor_tensor(stg[:, Q % 4, 1, :], psA[:, Q % 4, :],
                                                   stg[:, Q % 4, 0, :].bitcast(F32), ALU.subtract)
                        op.then_inc(q_lo, 1)
                for v in range(4):
                    dve.wait_ge(q_hi, 12 * i + (X_Q + 8 + v + 1))
                    for pr in range(2):
                        heads = [stg_v[:, v % 2, part, pr, :, :]
                                 .rearrange("p s (w n) -> p s w n", n=HD)[:, :, 0:3:2, :]
                                 for part in range(2)]
                        op = dve.tensor_tensor(
                            heads[1], psA[:, v, :].rearrange("p (s r w n) -> p s r w n", s=2, r=2, w=2)
                            [:, :, pr, :, :], heads[0].bitcast(F32), ALU.subtract)
                    op.then_inc(q_lo, 1)

            dve.wait_ge(tab_stored, 16)
            dve.wait_ge(gap_zeroed, 3)
            n_act = {("c", 0): 2, ("c", 1): 6}
            for c, (what, ch) in enumerate(CONV_ORDER):
                if what != "h":
                    continue
                for n in range(2):
                    dve.wait_ge(conv_done, 2 * c + n + 1)
                    dve.wait_ge(conv_act, n_act["c", ch] + n + 1)
                    cols = slice(n * HALF, (n + 1) * HALF)
                    dve.tensor_tensor(conv_u[:, 2 + n * HALF:2 + (n + 1) * HALF],
                                      psB[:, (2 * c + n) % 4, :], conv_c[:, cols], ALU.mult)\
                       .then_inc(conv_dve, 1)
                dve.wait_ge(conv_dve, 2 * ch + 2)
                chain(dve.tensor_scalar(conv_y, conv_u[:, 2:2 + S], conv_wt[:, 2, ch:ch + 1], None, ALU.mult))
                for tap in (1, 0):
                    chain(dve.scalar_tensor_tensor(out=conv_y, in0=conv_u[:, tap:tap + S],
                                                   scalar=conv_wt[:, tap, ch:ch + 1], in1=conv_y,
                                                   op0=ALU.mult, op1=ALU.add))
                dve.tensor_tensor(conv_out[:, ch, :], conv_y, conv_b[:, ch, :], ALU.mult)\
                   .then_inc(conv_ready, 1)
            gate_f, gate_e, cum = conv_c[0:GATES, :], conv_b[0:GATES, 0, :], conv_u[0:GATES, 0:S]
            dve.wait_ge(gate_step, 5)
            chain(dve.scalar_tensor_tensor(out=gate_f, in0=gate_f, scalar=0.0, in1=gate_e,
                                           op0=ALU.min, op1=ALU.subtract))
            dve.tensor_tensor_scan(cum, gate_f, gate_f, 0.0, ALU.add, ALU.bypass).then_inc(cum_ready, 1)

            def scores_min(s, a):
                if kind(s) == SB:
                    return
                pr, h, g = STEPS[s]
                t, W, i = 2 * s + a, width(s), 2 * g + a
                hd = 2 * pr + h
                z = psA[:, 2 * a:2 * a + 2, :].rearrange("p b n -> p (b n)")[:, 0:W]
                at = 896 - i * P if kind(s) == DIL else 0
                dve.wait_ge(z_ready, t + 1)
                if s >= 2:
                    dve.wait_ge(pt_ready, CUM[s - 1])
                if g == 0 and a == 0:
                    dve.wait_ge(bias_loaded[hd % 2], 16 * ((hd - 4) // 2 + 1))
                dve.tensor_tensor_reduce(out=probs[:, s % 2, a, 0:W], in0=z,
                                         in1=bias_t[:, h, at:at + W], scale=1.0, scalar=2 * MASKED,
                                         op0=ALU.add, op1=ALU.min,
                                         accum_out=negmax[:, t % 4:t % 4 + 1]).then_inc(z_read_dve, 1)

            def probabilities(s, a):
                t, W = 2 * s + a, width(s)
                p = probs[:, s % 2, a, 0:W]
                if kind(s) == SB:
                    r = rest[:, a, 0:W]
                    dve.wait_ge(z_read_act, t + 1)
                    dve.tensor_tensor_scan(r[:, ::-1], r[:, ::-1], r[:, ::-1], 1.0, ALU.mult, ALU.bypass)\
                       .then_inc(rest_scanned, 1)
                    dve.wait_ge(rest_scanned, t + 1)
                    dve.tensor_tensor(p[:, 0:W - 1], p[:, 0:W - 1], r[:, 1:W], ALU.mult)\
                       .then_inc(probs_ready, 1)
                else:
                    c = slice(t % 4, t % 4 + 1)
                    dve.wait_ge(exp_done, t - 32 + 1)
                    dve.reciprocal(rden[:, c], den[:, c]).then_inc(rden_ready, 1)
                    dve.wait_ge(rden_ready, t - 32 + 1)
                    dve.tensor_scalar(p, p, rden[:, c], None, ALU.mult).then_inc(probs_ready, 1)

            def transposed_lo(s, j):
                k = CUM[s] + j
                dve.wait_ge(pt_hi_done, k + 1)
                dve.tensor_tensor(pt_lo[:, k % 3, :, :].rearrange("p b n -> p (b n)"), psB[:, k % 2, :],
                                  pt_hi[:, k % 3, :, :].rearrange("p b n -> p (b n)").bitcast(F32),
                                  ALU.subtract).then_inc(pt_lo_done, 1)

            def mixed_lo(s):
                pr, h, g = STEPS[s]
                dve.wait_ge(o_hi, s + 1)
                lanes = slice(h * HD, (h + 1) * HD)
                dve.tensor_tensor(act_lo[lanes, pr, g * 256:(g + 1) * 256], psB[lanes, 2 + s % 2, 0:256],
                                  act_hi[lanes, pr, g * 256:(g + 1) * 256].bitcast(F32), ALU.subtract)\
                   .then_inc(o_lo, 1)

            for a in range(2):
                scores_min(0, a)
            for a in range(2):
                probabilities(0, a)
            for s in range(NS):
                g = STEPS[s][2]
                if s + 1 < NS:
                    scores_min(s + 1, 0)
                    scores_min(s + 1, 1)
                transposed_lo(s, 0)
                if s >= 1:
                    mixed_lo(s - 1)
                if g >= 1:
                    transposed_lo(s, 1)
                if s + 1 < NS:
                    probabilities(s + 1, 0)
                if g >= 2:
                    transposed_lo(s, 2)
                if s + 1 < NS:
                    probabilities(s + 1, 1)
                if g >= 3:
                    transposed_lo(s, 3)
            mixed_lo(NS - 1)

            ln_chained = [0]

            def ln_chain(op):
                ln_chained[0] += 1
                op.then_inc(ln_step, 1)
                dve.wait_ge(ln_step, ln_chained[0])

            def ln_moments(st):
                for n in range(2):
                    op = dve.bn_stats(stats[:, st % 2, n, :], y[:, st, n * HALF:(n + 1) * HALF])
                ln_chain(op)
                dve.bn_aggr(mv[:, st % 2, :], stats[:, st % 2, :, :]).then_inc(ln_stats, 1)

            def ln_finish(n, st):
                dve.wait_ge(ln_std, n + 1)
                dve.wait_ge(ln_stats, n + 1)
                ln_chain(dve.reciprocal(std[:, st % 2, 1:2], std[:, st % 2, 0:1]))
                ln_chain(dve.tensor_scalar(y[:, st, :], y[:, st, :], mv[:, st % 2, 0:1], std[:, st % 2, 1:2],
                                           ALU.subtract, ALU.mult))
                ln_chain(dve.tensor_tensor(y[:, st, :], y[:, st, :], gb[:, 0, :], ALU.mult))
                dve.tensor_tensor(y[:, st, :], y[:, st, :], gb[:, 1, :], ALU.add).then_inc(ln_done, 1)

            def x1_lo_part(st):
                for h in range(2):
                    q = 2 * st + h
                    part = (slice(None), slice(4 * h, 4 * h + 4), slice(st * P, (st + 1) * P))
                    dve.wait_ge(x1_hi, q + 1)
                    dve.tensor_tensor(act_lo[part], psB[:, q % 4, :].rearrange("p (k n) -> p k n", k=4),
                                      act_hi[part].bitcast(F32), ALU.subtract).then_inc(psb_drained, 1)

            for nh in range(2):
                for st in range(ST + (2 if nh else 0)):
                    if st < ST:
                        q = nh * ST + st
                        if nh == 0:
                            dve.wait_ge(res_loaded[st], 16)
                        dve.wait_ge(wo_done, q + 1)
                        yp = y[:, st, nh * HALF:(nh + 1) * HALF]
                        dve.scalar_tensor_tensor(out=yp, in0=yp, scalar=ALPHA, in1=psA[:, q % 4, :],
                                                 op0=ALU.mult, op1=ALU.add).then_inc(y_added, 1)
                        if nh == 1:
                            dve.wait_ge(y_added, q + 1)
                            ln_moments(st)
                    if nh == 1 and 1 <= st <= ST:
                        if st == 1:
                            dve.wait_ge(ln_rows, 32)
                        ln_finish(st - 1, st - 1)
                    if nh == 1 and st >= 2:
                        x1_lo_part(st - 2)

            def gated_unit(n_gu, par, ch):
                for n in range(2):
                    dve.wait_ge(silu_done, n_gu + n + 1)
                    if not (isinstance(n_gu, int) and n_gu == 0):
                        dve.wait_ge(hlo_done, n_gu + (n - 1))
                    dve.tensor_tensor(h_t[:, n, :], psA[:, 2 * n + 1, :], silu_t[:, n, :], ALU.mult)\
                       .then_inc(h_done, 1)
                for n in range(2):
                    cols = slice(n * HALF, (n + 1) * HALF)
                    dve.wait_ge(hhi_done, n_gu + n + 1)
                    dve.tensor_tensor(h_lo[:, par, ch, cols], h_t[:, n, :],
                                      h_hi[:, par, ch, cols].bitcast(F32), ALU.subtract).then_inc(hlo_done, 1)

            def add_down(n_dn, st, nh):
                q = 2 * st + nh
                dve.wait_ge(dn_done, n_dn + q + 1)
                yp = y[:, st, nh * HALF:(nh + 1) * HALF]
                dve.tensor_tensor(yp, yp, psB[:, q % 4, :], ALU.add).then_inc(psb_drained, 1)

            dve.wait_ge(x1_scaled, ST)
            gated_unit(0, 0, 0)
            gated_unit(2, 0, 1)
            with dve.Fori(0, (GROUPS - 1) // 2) as it:
                for j in range(2):
                    gated_unit(8 * it + (4 + 4 * j), (j + 1) % 2, 0)
                    for q in range(16):
                        add_down(32 * it + 16 * j, q // 2, q % 2)
                    gated_unit(8 * it + (4 + 4 * j + 2), (j + 1) % 2, 1)
            n_dn = 16 * (GROUPS - 1)
            dve.wait_ge(ln_rows, 64)
            for st in range(ST + 1):
                if st < ST:
                    for nh in range(2):
                        add_down(n_dn, st, nh)
                    dve.wait_ge(psb_drained, X_Q + n_dn + 2 * st + 2)
                    ln_moments(st)
                if st >= 1:
                    ln_finish(ST + st - 1, st - 1)

        @block.tensor
        def _(pe):
            def product(dst, w, v, first, last):
                pe.matmul(dst, w[0], v[0], start=first, stop=False)
                pe.matmul(dst, w[0], v[1], start=False, stop=False)
                return pe.matmul(dst, w[1], v[0], start=False, stop=last)

            def act_cols(k, cols):
                return act_hi[:, k, cols], act_lo[:, k, cols]

            pe.wait_ge(consts_ready, 2)
            for Q in range(X_Q):
                st, h = divmod(Q, 2)
                if h == 0:
                    pe.wait_ge(x_loaded[st % 4], 16 * (st // 4 + 1))
                if Q >= 4:
                    pe.wait_ge(q_lo, Q - 3)
                for k in range(4):
                    c = 4 * h + k
                    op = pe.transpose(psA[:, Q % 4, k * P:(k + 1) * P],
                                      x_tile[:, st % 4, c * P:(c + 1) * P], ident[:, :])
                op.then_inc(q_done, 1)

            def unit_w(slot):
                return [as_chunks(w[:, slot, :]) for w in (w_hi, w_lo)]

            def feature_major(dst, slot, n):
                w = unit_w(slot)
                for k in range(KC):
                    op = product(dst, (w[0][:, k, :], w[1][:, k, :]),
                                 act_cols(k, slice(n * HALF, (n + 1) * HALF)), k == 0, k == KC - 1)
                return op

            pe.wait_ge(q_lo, X_Q)
            with pe.Fori(0, 3) as i:
                for c in range(4):
                    pe.wait_ge(wlo_ready, 6 * i + (c + 1))
                    for n in range(2):
                        Q = 2 * c + n
                        pe.wait_ge(q_lo, 12 * i + (X_Q + Q - 3))
                        op = feature_major(psA[:, Q % 4, :], c % 3, n)
                        op.then_inc(q_done, 1)
                pe.wait_ge(wlo_ready, 6 * i + 6)
                for v in range(4):
                    pe.wait_ge(q_lo, 12 * i + (X_Q + 8 + v - 3))
                    for s2 in range(2):
                        st = 2 * v + s2
                        for k in range(KC):
                            slot = (4 + k // 4) % 3
                            w = [t[:, slot, (k % 4) * 256:(k % 4 + 1) * 256] for t in (w_hi, w_lo)]
                            op = product(psA[:, v, s2 * 256:(s2 + 1) * 256],
                                         act_cols(k, slice(st * P, (st + 1) * P)), w,
                                         k == 0, k == KC - 1)
                    op.then_inc(q_done, 1)

            bank_free = {4: (conv_act, 1), 5: (conv_act, 2), 6: (conv_act, 3), 7: (conv_act, 4),
                         8: (conv_act, 5), 9: (conv_act, 6), 10: (conv_dve, 1), 11: (conv_dve, 2),
                         12: (conv_act, 7), 13: (conv_act, 8)}
            for c in range(7):
                u = PROJ_UNITS + c
                pe.wait_ge(wlo_ready, u + 1)
                for n in range(2):
                    v = 2 * c + n
                    if v in bank_free:
                        pe.wait_ge(*bank_free[v])
                    feature_major(psB[:, v % 4, :], u % 3, n).then_inc(conv_done, 1)

            def scores(s):
                pr, h, g = STEPS[s]
                par, W = pr % 2, width(s)
                if h == 0 and g == 0:
                    pe.wait_ge(qkv_loaded[par], 16 * 7 * (pr // 2 + 1))
                if s == 0:
                    pe.wait_ge(consts_ready, 8)
                    pe.wait_ge(q_lo, X_Q + 3 * KIND_Q)
                for a in range(2):
                    t, i = 2 * s + a, 2 * g + a
                    if t >= 2:
                        if t - 2 < 32:
                            pe.wait_ge(z_read_act, t - 1)
                        else:
                            pe.wait_ge(z_read_dve, t - 2 - 32 + 1)
                    q = q_st[par][h][:, i * P:(i + 1) * P]
                    masked = kind(s) != DIL
                    for b, c0 in enumerate(range(0, W, HALF)):
                        n = min(HALF, W - c0)
                        last = c0 + n == W
                        z = psA[:, 2 * a + b, 0:n]
                        pe.matmul(z, q, kh_st[par][h][:, c0:c0 + n], start=True, stop=False)
                        op = pe.matmul(z, q, kl_st[par][h][:, c0:c0 + n], start=False,
                                       stop=not (masked and last))
                        if masked and last:
                            op = pe.matmul(psA[:, 2 * a + b, n - 256:n], ident_bf[:, :],
                                           masks[:, int(kind(s) == SB), a, :], start=False, stop=True)
                    op.then_inc(z_ready, 1)

            def transposes(s, j):
                k = CUM[s] + j
                if k >= 2:
                    pe.wait_ge(pt_lo_done, k - 1)
                else:
                    pe.wait_ge(conv_ready, 2)
                    pe.wait_ge(gate_step, 2)
                for a in range(2):
                    if j == 0:
                        pe.wait_ge(probs_ready, 2 * s + a + 1)
                    for b in range(2):
                        kb = 2 * j + b
                        op = pe.transpose(psB[:, k % 2, b * 256 + a * P:b * 256 + (a + 1) * P],
                                          probs[:, s % 2, a, kb * P:(kb + 1) * P], ident[:, :])
                op.then_inc(pt_ready, 1)

            def values(s, j):
                pr, h, g = STEPS[s]
                k = CUM[s] + j
                if j == 0 and s >= 2:
                    pe.wait_ge(o_lo, s - 1)
                pe.wait_ge(pt_lo_done, k + 1)
                for b in range(2):
                    v = [v_t[pr % 2][:, part, 2 * j + b, h * HD:h * HD + P] for part in range(2)]
                    op = product(psB[:, 2 + s % 2, 0:256], v, (pt_hi[:, k % 3, b, :], pt_lo[:, k % 3, b, :]),
                                 j == 0 and b == 0, j == g and b == 1)
                op.then_inc(pv_done, 1)

            scores(0)
            for s in range(NS):
                if s + 1 < NS:
                    scores(s + 1)
                g = STEPS[s][2]
                for j in range(g + 1):
                    transposes(s, j)
                    if j >= 1:
                        values(s, j - 1)
                values(s, g)

            pe.wait_ge(conv_split, 2)
            pe.wait_ge(o_lo, NS)
            pe.wait_ge(z_read_dve, 64)

            def x1_transposes(st):
                pe.wait_ge(ln_done, st + 1)
                for h in range(2):
                    q = 2 * st + h
                    if q >= 4:
                        pe.wait_ge(psb_drained, q - 3)
                    for k in range(4):
                        c = 4 * h + k
                        op = pe.transpose(psB[:, q % 4, k * P:(k + 1) * P], y[:, st, c * P:(c + 1) * P],
                                          ident[:, :])
                    op.then_inc(x1_t, 1)

            for nh in range(2):
                for st in range(ST + (2 if nh else 0)):
                    if st < ST:
                        q = nh * ST + st
                        if q >= 4:
                            pe.wait_ge(y_added, q - 3)
                        for k in range(KC):
                            u = 4 * nh + k // 2
                            if st == 0 and k % 2 == 0:
                                pe.wait_ge(w3lo_ready, u + 1)
                            w = [t[:, u % 6, (k % 2) * HALF:(k % 2 + 1) * HALF] for t in (w3_hi, w3_lo)]
                            op = product(psA[:, q % 4, :], act_cols(k, slice(st * P, (st + 1) * P)), w,
                                         k == 0, k == KC - 1)
                        op.then_inc(wo_done, 1)
                    if nh == 1 and st >= 2:
                        x1_transposes(st - 2)

            def gate_up(u, slot, n_gu):
                pe.wait_ge(w3lo_ready, u + 2)
                for n in range(2):
                    if not (isinstance(n_gu, int) and n_gu == 0):
                        pe.wait_ge(h_done, n_gu + (n - 1))
                    for m in range(2):
                        w = [as_chunks(t[:, slot + m, :]) for t in (w3_hi, w3_lo)]
                        for k in range(KC):
                            op = product(psA[:, 2 * n + m, :], (w[0][:, k, :], w[1][:, k, :]),
                                         act_cols(k, slice(n * HALF, (n + 1) * HALF)), k == 0, k == KC - 1)
                    op.then_inc(gu_done, 1)

            def down(u, slot, n_dn, par, n_h):
                pe.wait_ge(w3lo_ready, u + 2)
                pe.wait_ge(hlo_done, n_h)
                for q in range(16):
                    st, nh = divmod(q, 2)
                    pe.wait_ge(psb_drained, n_dn + (X_Q + q - 3))
                    for ch in range(2):
                        w = [t[:, slot + ch, nh * HALF:(nh + 1) * HALF] for t in (w3_hi, w3_lo)]
                        cols = slice(st * P, (st + 1) * P)
                        op = product(psB[:, q % 4, :], (h_hi[:, par, ch, cols], h_lo[:, par, ch, cols]), w,
                                     ch == 0, ch == 1)
                    op.then_inc(dn_done, 1)

            pe.wait_ge(psb_drained, X_Q)
            pe.wait_ge(y_added, 2 * ST)
            gate_up(8, 2, 0)
            gate_up(10, 4, 2)
            with pe.Fori(0, (GROUPS - 1) // 2) as it:
                for j in range(2):
                    at = 12 + 6 * j
                    gate_up(12 * it + at, 0, 8 * it + (4 + 4 * j))
                    down(12 * it + (at + 2), 2, 32 * it + 16 * j, j % 2, 8 * it + (4 + 4 * j))
                    gate_up(12 * it + (at + 4), 4, 8 * it + (4 + 4 * j + 2))
            down(72, 0, 16 * (GROUPS - 1), 0, 4 * GROUPS)


_NAMES = ["x", "w_in", "f_bias", "conv_w", "w_out", "rel_bias", "ln1_g", "ln1_b", "w_gate", "w_up",
          "w_down", "ln2_g", "ln2_b"]


def kernel(**inputs):
    import numpy as _np
    import concourse.bacc as _bacc
    from concourse import mybir as _mybir
    from concourse.bass_utils import run_bass_kernel_spmd as _run

    nc = _bacc.Bacc("TRN2", target_bir_lowering=False, num_devices=1)
    arrays, args = {}, []
    for name in _NAMES:
        a = _np.ascontiguousarray(inputs[name])
        arrays[f"in_{name}"] = a
        args.append(nc.dram_tensor(f"in_{name}", a.shape, _mybir.dt.from_np(a.dtype),
                                   kind="ExternalInput").ap())
    args.append(nc.dram_tensor("out_x", (1, S, D), F32, kind="ExternalOutput").ap())
    layer(nc, *args)
    r = _run(nc, [arrays], core_ids=[0])
    return r.results[0]["out_x"]
```

```python
from contextlib import ExitStack

import concourse.bass as bass
import numpy as np
from concourse import mybir

F32 = mybir.dt.float32
F32R = mybir.dt.float32r
BF16 = mybir.dt.bfloat16
ACT = mybir.ActivationFunctionType
ALU = mybir.AluOpType

P = 128
S = 1024
D = 1024
KC = D // P
ST = S // P
HALF = 512
HD = 64
SCALE = HD ** -0.5
FF = 2816
FC = FF // P
GROUPS = FC // 2
GATES = 4
W_KIND = 3 * 256
CONV0 = 3 * W_KIND
GATE0 = CONV0 + 3 * 256
ALPHA = 2.0 ** 0.25
EPS = 1e-5
MASKED = 1e30
BUCKETS, MAX_DIST = 32, 2048
SB, DIL, FOX = 0, 1, 2
VW = 192
TAB = 1279
TOEP = 1152


def bucket_starts():
    d = np.arange(S)
    exact = BUCKETS // 2
    nf = np.maximum(d, 1).astype(np.float32)
    large = exact + (np.log(nf / np.float32(exact)) / np.float32(np.log(MAX_DIST / exact))
                     * np.float32(BUCKETS - exact)).astype(np.int32)
    b = np.where(d < exact, d, np.minimum(large, BUCKETS - 1))
    return [(int(k), int(np.argmax(b == k))) for k in range(BUCKETS) if (b == k).any()]


def layer(nc, x, w_in, f_bias, conv_w, w_out, rel_bias, ln1_g, ln1_b, w_gate, w_up, w_down,
          ln2_g, ln2_b, out):
    x, out = x[0], out[0]
    w_in, w_out, w_gate, w_up, w_down = w_in[0], w_out[0], w_gate[0], w_up[0], w_down[0]

    qk_scr = nc.dram_tensor("qk_scr", [6, 2, P, 2, S], F32, kind="Internal").ap()
    v_scr = nc.dram_tensor("v_scr", [6, P, 2, ST, VW], F32, kind="Internal").ap()
    tab_scr = nc.dram_tensor("tab_scr", [4, P, TAB], F32, kind="Internal").ap()
    cum_scr = nc.dram_tensor("cum_scr", [4, S], F32, kind="Internal").ap()

    X_Q = 2 * ST
    KIND_Q = 12
    PROJ_UNITS = 6 * 3
    CONV_ORDER = [("b", 0), ("c", 0), ("b", 1), ("f", 0), ("h", 0), ("c", 1), ("h", 1)]
    CONV_COL = {"b": CONV0, "c": CONV0 + 256, "h": CONV0 + 512}
    STEPS = [(pr, h, g) for pr in range(6) for h in range(2) for g in range(4)]
    NS = len(STEPS)
    CUM = [0]
    for _, _, g in STEPS:
        CUM.append(CUM[-1] + g + 1)
    QUANTA = [(s, j) for s in range(NS) for j in range(STEPS[s][2] + 1)]

    def kind(s):
        return STEPS[s][0] // 2

    def width(s):
        return (2 * STEPS[s][2] + 2) * P

    persistent, early, attn, late = ExitStack(), ExitStack(), ExitStack(), ExitStack()
    with persistent:
        def sb(stack, name, shape, dt=F32):
            return stack.enter_context(nc.sbuf_tensor(name, shape, dt))

        def sem(name):
            return persistent.enter_context(nc.semaphore(name))

        act_hi = sb(persistent, "act_hi", [P, KC, S], F32R)
        act_lo = sb(persistent, "act_lo", [P, KC, S], F32R)
        ident = sb(persistent, "ident", [P, P])
        ident_bf = sb(persistent, "ident_bf", [P, P], BF16)
        eps_t = sb(persistent, "eps_t", [P, 1])

        to_attn = ExitStack()
        q_st, kh_st, kl_st, v_t = [], [], [], []

        def stacks(stack, par):
            for lst, nm in ((q_st, "q_st"), (kh_st, "kh_st"), (kl_st, "kl_st")):
                lst.append([sb(stack, f"{nm}{par}{h}", [P, S], F32R) for h in range(2)])
            v_t.append(sb(stack, f"v_t{par}", [P, 2, ST, VW], F32R))

        stacks(to_attn, 0)
        conv_out = sb(to_attn, "conv_out", [P, 2, S])
        masks = sb(to_attn, "masks", [P, 2, 2, 256], BF16)

        raw = sb(early, "raw", [P, 3, D])
        w_hi = sb(early, "w_hi", [P, 3, D], F32R)
        w_lo = sb(early, "w_lo", [P, 3, D], F32R)
        stg = sb(early, "stg", [P, 4, 2, HALF], F32R)
        stg_v = sb(early, "stg_v", [P, 2, 2, 2, 2, VW], F32R)
        scratch = sb(early, "scratch", [P, 4, D])
        conv_u = sb(early, "conv_u", [P, S + 2])
        gate_f = sb(early, "gate_f", [GATES, S])
        gate_e = sb(early, "gate_e", [GATES, S])
        conv_wt = sb(early, "conv_wt", [P, 3, 2])
        rel_t = sb(early, "rel_t", [4, BUCKETS])
        fb_t = sb(early, "fb_t", [4, 1])
        x_tile = scratch
        conv_b, conv_y, conv_c = scratch[:, 0:2, :], scratch[:, 2, :], scratch[:, 3, :]
        early.close()

        probs = sb(attn, "probs", [P, 3, 2, S])
        rest = [sb(attn, "rest", [P, 2, S]), conv_out]
        pt_hi = sb(attn, "pt_hi", [P, 3, 2, 256], F32R)
        pt_lo = sb(attn, "pt_lo", [P, 3, 2, 256], F32R)
        bias_t = sb(attn, "bias_t", [P, 2, TOEP])
        negmax = sb(attn, "negmax", [P, 8])
        den = sb(attn, "den", [P, 8])
        rden = sb(attn, "rden", [P, 8])
        stacks(attn, 1)
        attn.close()
        to_attn.close()

        raw3 = sb(late, "raw3", [P, 3, D])
        w3 = sb(late, "w3", [P, 6, 2, D], F32R)
        w3_hi, w3_lo = w3[:, :, 0, :], w3[:, :, 1, :]
        y = sb(late, "y", [P, ST, D])
        h_hi = sb(late, "h_hi", [P, 2, 2, S], F32R)
        h_lo = sb(late, "h_lo", [P, 2, 2, S], F32R)
        silu_t = sb(late, "silu_t", [P, 2, HALF])
        h_t = sb(late, "h_t", [P, 2, HALF])
        gb = sb(late, "gb", [P, 2, D])
        stats = sb(late, "stats", [P, 2, 2, 6])
        mv = sb(late, "mv", [P, 2, 2])
        std = sb(late, "std", [P, 2, 2])
        late.close()

        psA = persistent.enter_context(nc.psum_tensor("psA", [P, 4, HALF], F32))
        psB = persistent.enter_context(nc.psum_tensor("psB", [P, 4, HALF], F32))

        x_loaded = [sem(f"x_loaded{i}") for i in range(4)]
        small_loaded = sem("small_loaded")
        consts_ready = sem("consts_ready")
        raw_loaded = [sem(f"raw_loaded{i}") for i in range(3)]
        whi_ready, wlo_ready = sem("whi_ready"), sem("wlo_ready")
        q_done, q_hi, q_lo = sem("q_done"), sem("q_hi"), sem("q_lo")
        stored_qk = [sem(f"stored_qk{i}") for i in range(4)]
        stored_v = [sem(f"stored_v{i}") for i in range(2)]
        gap_zeroed = sem("gap_zeroed")
        tab_ready, tab_stored = sem("tab_ready"), sem("tab_stored")
        conv_done, conv_act, conv_dve = sem("conv_done"), sem("conv_act"), sem("conv_dve")
        conv_ready = sem("conv_ready")
        gate_step = sem("gate_step")
        cum_ready, cum_stored = sem("cum_ready"), sem("cum_stored")
        qkv_loaded = [sem("qkv_loaded0"), sem("qkv_loaded1")]
        bias_loaded = [sem("bias_loaded0"), sem("bias_loaded1")]
        z_ready, z_read_act, z_read_dve = sem("z_ready"), sem("z_read_act"), sem("z_read_dve")
        exp_done, rden_ready, probs_ready = sem("exp_done"), sem("rden_ready"), sem("probs_ready")
        rest_scanned = sem("rest_scanned")
        pt_ready, pt_hi_done, pt_lo_done = sem("pt_ready"), sem("pt_hi_done"), sem("pt_lo_done")
        pv_done, o_hi, o_lo = sem("pv_done"), sem("o_hi"), sem("o_lo")
        conv_split = sem("conv_split")
        raw3_loaded = [sem(f"raw3_loaded{i}") for i in range(3)]
        w3hi_ready, w3lo_ready = sem("w3hi_ready"), sem("w3lo_ready")
        res_loaded, ln_rows = [sem(f"res_loaded{i}") for i in range(ST)], sem("ln_rows")
        wo_done, y_added = sem("wo_done"), sem("y_added")
        ln_stats, ln_std, ln_step, ln_done = sem("ln_stats"), sem("ln_std"), sem("ln_step"), sem("ln_done")
        x1_t, x1_hi, x1_scaled = sem("x1_t"), sem("x1_hi"), sem("x1_scaled")
        gu_done, silu_done, h_done = sem("gu_done"), sem("silu_done"), sem("h_done")
        hhi_done, hlo_done = sem("hhi_done"), sem("hlo_done")
        dn_done, psb_drained = sem("dn_done"), sem("psb_drained")
        stored = sem("stored")
        dve_step = sem("dve_step")

        def in_unit(col):
            return w_in[:, col].rearrange("(k p) n -> p k n", p=P)

        def as_chunks(slot):
            return slot.rearrange("p (k n) -> p k n", k=KC)

        block = persistent.enter_context(nc.Block())

        @block.sync
        def _(sp):
            for st in range(4):
                sp.dma_start(x_tile[:, st, :], x[st * P:(st + 1) * P, :]).then_inc(x_loaded[st], 16)
            sp.dma_start(rel_t[:, :], rel_bias.rearrange("b h -> h b"), allow_slow_non_contiguous=True).then_inc(small_loaded, 16)
            sp.dma_start(fb_t[:, :], f_bias.rearrange("a h -> h a"), allow_slow_non_contiguous=True).then_inc(small_loaded, 16)
            sp.dma_start(conv_wt[:, :, :], conv_w[0].rearrange("j (c p) -> p j c", p=P),
                         allow_slow_non_contiguous=True)\
              .then_inc(small_loaded, 16)

            QK_COL = [0, 256, 128, 384]

            def load_qk(col, slot):
                sp.dma_start(as_chunks(raw[:, slot, :]), in_unit(col)).then_inc(raw_loaded[slot], 16)

            def load_v(kind_i, half, slot):
                rows = w_in[half * HALF:(half + 1) * HALF, bass.ds(kind_i * W_KIND + 512, 256)]
                sp.dma_start(raw[:, slot, :].rearrange("p (k n) -> p k n", k=4),
                             rows.rearrange("(k p) n -> p k n", p=P)).then_inc(raw_loaded[slot], 16)

            for c in range(3):
                load_qk(slice(QK_COL[c], QK_COL[c] + P), c)
            for st in range(4, ST):
                sp.wait_ge(q_done, 2 * (st - 3))
                sp.dma_start(x_tile[:, st % 4, :], x[st * P:(st + 1) * P, :])\
                  .then_inc(x_loaded[st % 4], 16)
            sp.wait_ge(tab_ready, 1)
            tab_row = conv_out[0:4].rearrange("p a n -> p (a n)")[:, 0:TAB]
            sp.dma_start(tab_scr, tab_row.unsqueeze(1).broadcast_to([4, P, TAB])).then_inc(tab_stored, 16)

            with sp.Fori(0, 3) as i:
                for c in range(6):
                    sp.wait_ge(whi_ready, 6 * i + (c + 1))
                    sp.wait_ge(wlo_ready, 6 * i + (c + 1))
                    if c == 0:
                        load_qk(bass.ds(i * W_KIND + QK_COL[3], P), 0)
                    elif c < 3:
                        load_v(i, c - 1, c)
                    else:
                        load_qk(bass.ds(i * W_KIND + (W_KIND + QK_COL[c - 3]), P), c - 3)
                    if c < 4:
                        for n in range(2):
                            sp.wait_ge(q_lo, 12 * i + (X_Q + 2 * c + n + 1))
                            slot = (2 * c + n) % 4
                            sp.dma_start(
                                qk_scr[bass.ds(2 * i + c // 2, 1), c % 2, :, :, n * HALF:(n + 1) * HALF]
                                .rearrange("a p t n -> (a p) t n"),
                                stg[:, slot, :, :].bitcast(F32)).then_inc(stored_qk[slot], 16)
                    elif c == 5:
                        for v in range(4):
                            sp.wait_ge(q_lo, 12 * i + (X_Q + 8 + v + 1))
                            for pr in range(2):
                                sp.dma_start(
                                    v_scr[bass.ds(2 * i + pr, 1), :, :, 2 * v:2 * v + 2, :]
                                    .rearrange("a p t s n -> (a p) t (s n)"),
                                    stg_v[:, v % 2, :, pr, :, :].rearrange("p t s n -> p t (s n)").bitcast(F32))\
                                  .then_inc(stored_v[v % 2], 16)
            for c in range(3, 7):
                u = PROJ_UNITS + c
                sp.wait_ge(whi_ready, u - 2)
                sp.wait_ge(wlo_ready, u - 2)
                what, ch = CONV_ORDER[c]
                if what == "f":
                    dst = as_chunks(raw[:, u % 3, :])
                    sp.dma_start(dst[:, :, 0:GATES], in_unit(slice(GATE0, GATE0 + GATES)))\
                      .then_inc(raw_loaded[u % 3], 16)
                    sp.dma_start(dst[:, :, GATES:P], in_unit(slice(0, P - GATES)))\
                      .then_inc(raw_loaded[u % 3], 16)
                else:
                    col = CONV_COL[what] + ch * P
                    load_qk(slice(col, col + P), u % 3)

            for k in range(4):
                sp.wait_ge(stored_qk[k], 16 * 6)
            for k in range(2):
                sp.wait_ge(stored_v[k], 16 * 12)

            def load_pair(pr):
                par = pr % 2
                for h in range(2):
                    for which, part, stride, dst in ((0, 0, S, q_st), (1, 0, 0, kh_st), (1, 1, 0, kl_st)):
                        at = ((pr * 2 + which) * P + h * HD) * 2 * S + part * S
                        sp.dma_start(dst[par][h][:, :].bitcast(F32),
                                     bass.AP(qk_scr.tensor, at, [[stride, 2], [2 * S, HD], [1, S]]))\
                          .then_inc(qkv_loaded[par], 16)
                sp.dma_start(v_t[par][:, :, :, :].bitcast(F32), v_scr[pr]).then_inc(qkv_loaded[par], 16)

            def load_bias(hd):
                if hd < 8:
                    src = bass.AP(tab_scr.tensor, (hd - 4) * P * TAB + P - 1, [[TAB - 1, P], [1, TOEP]])
                    dst = bias_t[:, hd % 2, :]
                else:
                    src = bass.AP(cum_scr.tensor, (hd - 8) * S, [[0, P], [1, S]])
                    dst = bias_t[:, hd % 2, 0:S]
                sp.dma_start(dst, src).then_inc(bias_loaded[hd % 2], 16)

            load_pair(0)
            sp.wait_ge(tab_stored, 16)
            sp.wait_ge(cum_ready, 1)
            sp.dma_start(cum_scr, gate_e[:, :]).then_inc(cum_stored, 16)
            sp.wait_ge(cum_stored, 16)
            sp.wait_ge(conv_ready, 2)
            load_pair(1)
            load_bias(4)
            load_bias(5)
            for pr in range(2, 6):
                sp.wait_ge(pv_done, CUM[8 * (pr - 1)])
                load_pair(pr)
                for hd in (2 * pr, 2 * pr + 1) if pr > 2 else ():
                    sp.wait_ge(z_read_dve, 8 * (hd - 2 - 4) + 8)
                    load_bias(hd)

            sp.wait_ge(pv_done, CUM[8 * 5])

            def slot_free(u):
                if isinstance(u, int) and u < 3:
                    return
                sp.wait_ge(w3hi_ready, u - 2)
                sp.wait_ge(w3lo_ready, u - 2)

            for u in range(8):
                if u == 6:
                    sp.wait_ge(o_lo, NS)
                    sp.wait_ge(conv_split, 2)
                    for st in range(ST):
                        sp.dma_start(y[:, st, :], x[st * P:(st + 1) * P, :])\
                          .then_inc(res_loaded[st], 16)
                    for k, row in enumerate((ln1_g, ln1_b)):
                        sp.dma_start(gb[:, k, :], bass.AP(row.tensor, 0, [[0, P], [1, D]]))\
                          .then_inc(ln_rows, 16)
                slot_free(u)
                nh, kp = divmod(u, 4)
                src = w_out[2 * kp * P:(2 * kp + 2) * P, nh * HALF:(nh + 1) * HALF]
                sp.dma_start(raw3[:, u % 3, :].rearrange("p (k n) -> p k n", k=2),
                             src.rearrange("(k p) n -> p k n", p=P)).then_inc(raw3_loaded[u % 3], 16)

            def load_gu(u, slot, w, chunk):
                slot_free(u)
                sp.dma_start(as_chunks(raw3[:, slot, :]),
                             w[:, bass.ds(chunk * P, P)].rearrange("(k p) n -> p k n", p=P))\
                  .then_inc(raw3_loaded[slot], 16)

            def load_dn(u, slot, chunk):
                slot_free(u)
                sp.dma_start(raw3[:, slot, :], w_down[bass.ds(chunk * P, P), :])\
                  .then_inc(raw3_loaded[slot], 16)

            for c in range(2):
                load_gu(8 + 2 * c, (8 + 2 * c) % 3, w_gate, c)
                load_gu(9 + 2 * c, (9 + 2 * c) % 3, w_up, c)
            with sp.Fori(0, (GROUPS - 1) // 2) as it:
                for j in range(2):
                    at = 12 + 6 * j
                    load_gu(12 * it + at, at % 3, w_gate, 4 * it + (2 * j + 2))
                    load_gu(12 * it + (at + 1), (at + 1) % 3, w_up, 4 * it + (2 * j + 2))
                    load_dn(12 * it + (at + 2), (at + 2) % 3, 4 * it + 2 * j)
                    load_dn(12 * it + (at + 3), (at + 3) % 3, 4 * it + (2 * j + 1))
                    load_gu(12 * it + (at + 4), (at + 4) % 3, w_gate, 4 * it + (2 * j + 3))
                    load_gu(12 * it + (at + 5), (at + 5) % 3, w_up, 4 * it + (2 * j + 3))
            load_dn(72, 0, FC - 2)
            load_dn(73, 1, FC - 1)
            sp.wait_ge(ln_done, ST)
            for k, row in enumerate((ln2_g, ln2_b)):
                sp.dma_start(gb[:, k, :], bass.AP(row.tensor, 0, [[0, P], [1, D]]))\
                  .then_inc(ln_rows, 16)
            for st in range(ST):
                sp.wait_ge(ln_done, ST + st + 1)
                sp.dma_start(out[st * P:(st + 1) * P, :], y[:, st, :]).then_inc(stored, 16)
            sp.wait_ge(stored, 16 * ST)

        @block.gpsimd
        def _(pool):
            pool.memset(ident[:, :], 0.0).then_inc(consts_ready, 1)
            pool.wait_ge(consts_ready, 1)
            pool.affine_select(out=ident[:, :], in_=ident[:, :], compare_op=ALU.not_equal, fill=1.0,
                               base=0, pattern=[[-1, P]], channel_multiplier=1).then_inc(consts_ready, 1)
            pool.memset(stg_v[:, :, :, :, :, HD:P].rearrange("p s t r k n -> p (s t r k) n").bitcast(F32),
                        0.0).then_inc(gap_zeroed, 1)
            pool.memset(conv_u[:, 0:2], 0.0).then_inc(gap_zeroed, 1)
            pool.memset(eps_t[:, :], EPS).then_inc(gap_zeroed, 1)
            pool.wait_ge(consts_ready, 2)
            pool.tensor_copy(ident_bf[:, :], ident[:, :]).then_inc(consts_ready, 1)
            pool.memset(masks[:, :, :, :].rearrange("p a b n -> p (a b n)"), 0.0).then_inc(consts_ready, 1)
            pool.wait_ge(consts_ready, 4)
            for strict in range(2):
                for a in range(2):
                    m = masks[:, strict, a, :]
                    pool.affine_select(out=m, in_=m, compare_op=ALU.is_gt if strict else ALU.is_ge,
                                       fill=MASKED, base=a * P, pattern=[[-1, 256]],
                                       channel_multiplier=1).then_inc(consts_ready, 1)

            def split_lo(u, slot, n_loaded):
                pool.wait_ge(raw_loaded[slot], n_loaded)
                pool.wait_ge(whi_ready, u + 1)
                pool.tensor_tensor(w_lo[:, slot, :], raw[:, slot, :], w_hi[:, slot, :].bitcast(F32),
                                   ALU.subtract).then_inc(wlo_ready, 1)

            with pool.Fori(0, 3) as i:
                for c in range(6):
                    split_lo(6 * i + c, c % 3, 32 * i + 16 * (c // 3 + 1))
            for c in range(7):
                u = PROJ_UNITS + c
                split_lo(u, u % 3, 16 * (u // 3 + 1) + 16 * (c >= 3 and u % 3 == 0))

            for ch in range(2):
                pool.wait_ge(q_hi, X_Q + 3 * KIND_Q + ch + 1)
                pool.tensor_tensor(act_lo[:, 6 + ch, :], conv_out[:, ch, :],
                                   act_hi[:, 6 + ch, :].bitcast(F32), ALU.subtract).then_inc(conv_split, 1)

            def probabilities(s, a):
                t, W = 2 * s + a, width(s)
                p = probs[:, s % 3, a, 0:W]
                if kind(s) == SB:
                    pool.wait_ge(rest_scanned, t + 1)
                    pool.tensor_tensor(p[:, 0:W - 1], p[:, 0:W - 1], rest[s % 2][:, a, 1:W], ALU.mult)\
                        .then_inc(probs_ready, 1)
                else:
                    pool.wait_ge(rden_ready, t - 32 + 1)
                    pool.tensor_tensor(p, p, rden[:, t % 8:t % 8 + 1].broadcast_to([P, W]), ALU.mult)\
                        .then_inc(probs_ready, 1)

            def split3_lo(u, slot, n_loaded):
                pool.wait_ge(raw3_loaded[slot % 3], n_loaded)
                pool.wait_ge(w3hi_ready, u + 1)
                pool.tensor_tensor(w3_lo[:, slot, :], raw3[:, slot % 3, :], w3_hi[:, slot, :].bitcast(F32),
                                   ALU.subtract).then_inc(w3lo_ready, 1)

            for s in range(NS):
                for a in range(2):
                    probabilities(s, a)
                if s >= NS - 4 and s < NS - 1:
                    split3_lo(s - NS + 4, s - NS + 4, 16)

            for u in range(3, 12):
                split3_lo(u, u % 6, 16 * (u // 3 + 1))
            with pool.Fori(0, (GROUPS - 1) // 2) as it:
                for c in range(12):
                    split3_lo(12 * it + (12 + c), c % 6, 64 * it + 16 * (4 + c // 3 + 1))
            for u in (72, 73):
                split3_lo(u, u % 6, 16 * (u // 3 + 1))

        @block.scalar
        def _(act):
            def split_hi(slot, n_loaded):
                act.wait_ge(raw_loaded[slot], n_loaded)
                act.activation(w_hi[:, slot, :], raw[:, slot, :], ACT.Copy).then_inc(whi_ready, 1)

            for Q in range(X_Q):
                st, h = divmod(Q, 2)
                if Q in (6, 8, 10):
                    split_hi(Q // 2 - 3, 16)
                act.wait_ge(q_done, Q + 1)
                act.activation(act_hi[:, 4 * h:4 * h + 4, st * P:(st + 1) * P],
                               psA[:, Q % 4, :].rearrange("p (k n) -> p k n", k=4), ACT.Copy)\
                   .then_inc(q_hi, 1)

            act.wait_ge(gap_zeroed, 1)
            with act.Fori(0, 3) as i:
                for c in range(6):
                    if c < 4:
                        for n in range(2):
                            Q = 2 * c + n
                            act.wait_ge(q_done, 12 * i + (X_Q + Q + 1))
                            if Q >= 4:
                                act.wait_ge(stored_qk[Q % 4], 32 * i + 16)
                            act.activation(stg[:, Q % 4, 0, :], psA[:, Q % 4, :], ACT.Copy,
                                           scale=-SCALE if c % 2 == 0 else 1.0).then_inc(q_hi, 1)
                    elif c == 5:
                        for v in range(4):
                            act.wait_ge(q_done, 12 * i + (X_Q + 8 + v + 1))
                            if v >= 2:
                                act.wait_ge(stored_v[v % 2], 64 * i + 32)
                            for pr in range(2):
                                op = act.activation(
                                    stg_v[:, v % 2, 0, pr, :, :]
                                    .rearrange("p s (w n) -> p s w n", n=HD)[:, :, 0:3:2, :],
                                    psA[:, v, :].rearrange("p (s r w n) -> p s r w n", s=2, r=2, w=2)
                                    [:, :, pr, :, :], ACT.Copy)
                            op.then_inc(q_hi, 1)
                    for d in {4: (), 5: (4, 5)}.get(c, (c,)):
                        split_hi(d % 3, 32 * i + 16 * ((d + 3) // 3 + 1))
                for k in range(4):
                    act.wait_ge(stored_qk[k], 32 * i + 32)
                for k in range(2):
                    act.wait_ge(stored_v[k], 64 * i + 64)

            act.wait_ge(tab_ready, 1)
            for c, (what, ch) in enumerate(CONV_ORDER):
                for n in range(2):
                    if what == "h":
                        continue
                    act.wait_ge(conv_done, 2 * c + n + 1)
                    cols, bank = slice(n * HALF, (n + 1) * HALF), psB[:, (2 * c + n) % 4, :]
                    if what == "f":
                        act.activation(gate_f[:, cols], bank[0:GATES], ACT.Identity,
                                       bias=fb_t[:, 0:1]).then_inc(gate_step, 1)
                        continue
                    if (what, ch, n) == ("c", 1, 0):
                        act.wait_ge(conv_dve, 2)
                    act.activation(conv_b[:, ch, cols] if what == "b" else conv_c[:, cols], bank,
                                   ACT.Copy).then_inc(conv_act, 1)
                if what == "f":
                    act.wait_ge(gate_step, 2)
                    act.activation(gate_e[:, :], gate_f[:, :], ACT.Abs).then_inc(gate_step, 1)
                    act.wait_ge(gate_step, 3)
                    act.activation(gate_e[:, :], gate_e[:, :], ACT.Exp, scale=-1.0).then_inc(gate_step, 1)
                    act.wait_ge(gate_step, 4)
                    act.activation(gate_e[:, :], gate_e[:, :], ACT.Ln, bias=1.0).then_inc(gate_step, 1)
                if c + 3 < len(CONV_ORDER):
                    u = PROJ_UNITS + c + 3
                    act.wait_ge(conv_done, 2 * c + 2)
                    split_hi(u % 3, 16 * (u // 3 + 1) + 16 * (u % 3 == 0))

            for ch in range(2):
                act.wait_ge(conv_ready, ch + 1)
                act.wait_ge(conv_done, 2 * len(CONV_ORDER))
                act.activation(act_hi[:, 6 + ch, :], conv_out[:, ch, :], ACT.Copy).then_inc(q_hi, 1)

            def softmax_part(s, a):
                t, W = 2 * s + a, width(s)
                p = probs[:, s % 3, a, 0:W]
                if kind(s) == SB:
                    z = psA[:, 2 * a:2 * a + 2, :].rearrange("p b n -> p (b n)")[:, 0:W]
                    if s >= 3:
                        act.wait_ge(pt_ready, CUM[s - 2])
                    act.wait_ge(z_ready, t + 1)
                    act.activation(p, z, ACT.Sigmoid, scale=-1.0)
                    if s >= 2:
                        act.wait_ge(probs_ready, t - 3)
                    elif s == 1:
                        act.wait_ge(conv_split, 2)
                    act.activation(rest[s % 2][:, a, 0:W], z, ACT.Sigmoid).then_inc(z_read_act, 1)
                else:
                    act.wait_ge(z_read_dve, t - 32 + 1)
                    act.activation(p, p, ACT.Exp, bias=negmax[:, t % 8:t % 8 + 1], scale=-1.0,
                                   accum_out=den[:, t % 8:t % 8 + 1]).then_inc(exp_done, 1)

            def transposed_hi(s, j):
                k = CUM[s] + j
                act.wait_ge(pt_ready, k + 1)
                if k >= 3:
                    act.wait_ge(pv_done, k - 2)
                act.activation(pt_hi[:, k % 3, :, :].rearrange("p b n -> p (b n)"), psB[:, k % 2, :],
                               ACT.Copy).then_inc(pt_hi_done, 1)

            def mixed_hi(s):
                pr, h, g = STEPS[s]
                act.wait_ge(pv_done, CUM[s + 1])
                lanes = slice(h * HD, (h + 1) * HD)
                act.activation(act_hi[lanes, pr, g * 256:(g + 1) * 256], psB[lanes, 2 + s % 2, 0:256],
                               ACT.Copy).then_inc(o_hi, 1)

            def split3_hi(slot, n_loaded):
                act.wait_ge(raw3_loaded[slot % 3], n_loaded)
                act.activation(w3_hi[:, slot, :], raw3[:, slot % 3, :], ACT.Copy).then_inc(w3hi_ready, 1)

            for s in range(2):
                for a in range(2):
                    softmax_part(s, a)
            for k, (s, j) in enumerate(QUANTA):
                g = STEPS[s][2]
                transposed_hi(s, j)
                for a in range(2):
                    if s + 2 < NS and j == min(a + 1, g):
                        softmax_part(s + 2, a)
                for r in range(NS):
                    if CUM[r + 1] + 1 == k:
                        mixed_hi(r)
                if j == g and NS - 5 <= s < NS - 2:
                    split3_hi(s - NS + 5, 16)
            mixed_hi(NS - 1)

            def split3(u):
                if u >= 6:
                    act.wait_ge(wo_done, ST if u < 10 else 2 * ST)
                split3_hi(u % 6, 16 * (u // 3 + 1))

            def ln_root(n, st):
                act.wait_ge(ln_stats, n + 1)
                act.activation(std[:, st % 2, 0:1], mv[:, st % 2, 1:2], ACT.Sqrt, bias=eps_t[:, 0:1])\
                   .then_inc(ln_std, 1)

            def x1_hi_part(st):
                for h in range(2):
                    q = 2 * st + h
                    act.wait_ge(x1_t, q + 1)
                    act.activation(act_hi[:, 4 * h:4 * h + 4, st * P:(st + 1) * P],
                                   psB[:, q % 4, :].rearrange("p (k n) -> p k n", k=4), ACT.Copy)\
                       .then_inc(x1_hi, 1)
                act.activation(y[:, st, :], y[:, st, :], ACT.Copy, scale=ALPHA).then_inc(x1_scaled, 1)

            for u in range(3, 10):
                split3(u)
            for st in range(ST + 2):
                if st < ST:
                    ln_root(st, st)
                if st >= 2:
                    x1_hi_part(st - 2)
            for u in range(10, 14):
                split3(u)

            def gated_unit(n_gu, par, ch):
                for n in range(2):
                    act.wait_ge(gu_done, n_gu + n + 1)
                    act.activation(silu_t[:, n, :], psA[:, 2 * n, :], ACT.Silu).then_inc(silu_done, 1)
                for n in range(2):
                    act.wait_ge(h_done, n_gu + n + 1)
                    act.activation(h_hi[:, par, ch, n * HALF:(n + 1) * HALF], h_t[:, n, :], ACT.Copy)\
                       .then_inc(hhi_done, 1)

            gated_unit(0, 0, 0)
            gated_unit(2, 0, 1)
            with act.Fori(0, (GROUPS - 1) // 2) as it:
                for j in range(2):
                    for m in range(3):
                        for c in range(2):
                            u = 12 + 6 * j + 2 * m + 2 + c
                            split3_hi(u % 6, 64 * it + 16 * (u // 3 + 1))
                        if m != 1:
                            gated_unit(8 * it + (4 + 4 * j + m), (j + 1) % 2, m // 2)
            for st in range(ST):
                ln_root(ST + st, st)

        @block.vector
        def _(dve):
            chained = [0]

            def chain(op):
                chained[0] += 1
                op.then_inc(dve_step, 1)
                dve.wait_ge(dve_step, chained[0])

            for Q in range(X_Q):
                st, h = divmod(Q, 2)
                part = (slice(None), slice(4 * h, 4 * h + 4), slice(st * P, (st + 1) * P))
                dve.wait_ge(q_hi, Q + 1)
                dve.tensor_tensor(act_lo[part], psA[:, Q % 4, :].rearrange("p (k n) -> p k n", k=4),
                                  act_hi[part].bitcast(F32), ALU.subtract).then_inc(q_lo, 1)

            tab = conv_out[0:4].rearrange("p a n -> p (a n)")[:, 0:TAB]
            base = conv_u[0:4, 2:2 + S]
            dve.wait_ge(small_loaded, 48)
            chain(dve.memset(base, 0.0))
            chain(dve.memset(tab, MASKED))
            starts = bucket_starts()
            for n, (b, d0) in enumerate(starts):
                d1 = starts[n + 1][1] if n + 1 < len(starts) else S
                seg = base[:, S - d1:S - d0]
                op = dve.scalar_tensor_tensor(out=seg, in0=seg, scalar=rel_t[:, b:b + 1], in1=seg,
                                              op0=ALU.subtract, op1=ALU.add)
            chain(op)
            for lo, hi, step, count in ((0, 128, 1, 1), (0, 128, 4, 2), (0, 128, 16, 3),
                                        (132, 512, 4, 1), (144, 512, 16, 2), (528, 1008, 16, 1)):
                sel = slice(S - 1 - hi, S - lo, step)
                chain(dve.tensor_scalar(tab[:, sel], base[:, sel], -float(np.log(count)), None, ALU.add))
            dve.memset(base, 0.0).then_inc(tab_ready, 1)

            dve.wait_ge(gap_zeroed, 1)
            with dve.Fori(0, 3) as i:
                for c in range(4):
                    for n in range(2):
                        Q = 2 * c + n
                        dve.wait_ge(q_hi, 12 * i + (X_Q + Q + 1))
                        if c % 2 == 0:
                            op = dve.scalar_tensor_tensor(
                                out=stg[:, Q % 4, 1, :], in0=psA[:, Q % 4, :], scalar=-SCALE,
                                in1=stg[:, Q % 4, 0, :].bitcast(F32), op0=ALU.mult, op1=ALU.subtract)
                        else:
                            op = dve.tensor_tensor(stg[:, Q % 4, 1, :], psA[:, Q % 4, :],
                                                   stg[:, Q % 4, 0, :].bitcast(F32), ALU.subtract)
                        op.then_inc(q_lo, 1)
                for v in range(4):
                    dve.wait_ge(q_hi, 12 * i + (X_Q + 8 + v + 1))
                    for pr in range(2):
                        heads = [stg_v[:, v % 2, part, pr, :, :]
                                 .rearrange("p s (w n) -> p s w n", n=HD)[:, :, 0:3:2, :]
                                 for part in range(2)]
                        op = dve.tensor_tensor(
                            heads[1], psA[:, v, :].rearrange("p (s r w n) -> p s r w n", s=2, r=2, w=2)
                            [:, :, pr, :, :], heads[0].bitcast(F32), ALU.subtract)
                    op.then_inc(q_lo, 1)

            dve.wait_ge(tab_stored, 16)
            dve.wait_ge(gap_zeroed, 3)
            n_act = {("c", 0): 2, ("c", 1): 6}
            for c, (what, ch) in enumerate(CONV_ORDER):
                if what == "f":
                    dve.wait_ge(gate_step, 5)
                    chain(dve.scalar_tensor_tensor(out=gate_f[:, :], in0=gate_f[:, :], scalar=0.0,
                                                   in1=gate_e[:, :], op0=ALU.min, op1=ALU.subtract))
                    dve.tensor_tensor_scan(gate_e[:, :], gate_f[:, :], gate_f[:, :], 0.0, ALU.add,
                                           ALU.bypass).then_inc(cum_ready, 1)
                if what != "h":
                    continue
                for n in range(2):
                    dve.wait_ge(conv_done, 2 * c + n + 1)
                    dve.wait_ge(conv_act, n_act["c", ch] + n + 1)
                    cols = slice(n * HALF, (n + 1) * HALF)
                    dve.tensor_tensor(conv_u[:, 2 + n * HALF:2 + (n + 1) * HALF],
                                      psB[:, (2 * c + n) % 4, :], conv_c[:, cols], ALU.mult)\
                       .then_inc(conv_dve, 1)
                dve.wait_ge(conv_dve, 2 * ch + 2)
                chain(dve.tensor_scalar(conv_y, conv_u[:, 2:2 + S], conv_wt[:, 2, ch:ch + 1], None, ALU.mult))
                for tap in (1, 0):
                    chain(dve.scalar_tensor_tensor(out=conv_y, in0=conv_u[:, tap:tap + S],
                                                   scalar=conv_wt[:, tap, ch:ch + 1], in1=conv_y,
                                                   op0=ALU.mult, op1=ALU.add))
                dve.tensor_tensor(conv_out[:, ch, :], conv_y, conv_b[:, ch, :], ALU.mult)\
                   .then_inc(conv_ready, 1)

            def scores_min(s, a):
                if kind(s) == SB:
                    return
                pr, h, g = STEPS[s]
                t, W, i = 2 * s + a, width(s), 2 * g + a
                hd = 2 * pr + h
                z = psA[:, 2 * a:2 * a + 2, :].rearrange("p b n -> p (b n)")[:, 0:W]
                at = 896 - i * P if kind(s) == DIL else 0
                dve.wait_ge(z_ready, t + 1)
                dve.wait_ge(pt_ready, CUM[s - 2])
                if g == 0 and a == 0:
                    dve.wait_ge(bias_loaded[hd % 2], 16 * ((hd - 4) // 2 + 1))
                dve.tensor_tensor_reduce(out=probs[:, s % 3, a, 0:W], in0=z,
                                         in1=bias_t[:, h, at:at + W], scale=1.0, scalar=2 * MASKED,
                                         op0=ALU.add, op1=ALU.min,
                                         accum_out=negmax[:, t % 8:t % 8 + 1]).then_inc(z_read_dve, 1)

            def shares(s, a):
                t, W = 2 * s + a, width(s)
                if kind(s) == SB:
                    r = rest[s % 2][:, a, 0:W]
                    dve.wait_ge(z_read_act, t + 1)
                    dve.tensor_tensor_scan(r[:, ::-1], r[:, ::-1], r[:, ::-1], 1.0, ALU.mult, ALU.bypass)\
                       .then_inc(rest_scanned, 1)
                else:
                    c = slice(t % 8, t % 8 + 1)
                    dve.wait_ge(exp_done, t - 32 + 1)
                    dve.reciprocal(rden[:, c], den[:, c]).then_inc(rden_ready, 1)

            def transposed_lo(s, j):
                k = CUM[s] + j
                dve.wait_ge(pt_hi_done, k + 1)
                dve.tensor_tensor(pt_lo[:, k % 3, :, :].rearrange("p b n -> p (b n)"), psB[:, k % 2, :],
                                  pt_hi[:, k % 3, :, :].rearrange("p b n -> p (b n)").bitcast(F32),
                                  ALU.subtract).then_inc(pt_lo_done, 1)

            def mixed_lo(s):
                pr, h, g = STEPS[s]
                dve.wait_ge(o_hi, s + 1)
                lanes = slice(h * HD, (h + 1) * HD)
                dve.tensor_tensor(act_lo[lanes, pr, g * 256:(g + 1) * 256], psB[lanes, 2 + s % 2, 0:256],
                                  act_hi[lanes, pr, g * 256:(g + 1) * 256].bitcast(F32), ALU.subtract)\
                   .then_inc(o_lo, 1)

            for a in range(2):
                shares(0, a)
            for k, (s, j) in enumerate(QUANTA):
                g = STEPS[s][2]
                transposed_lo(s, j)
                for a in range(2):
                    if j == min(a, g):
                        if s + 1 < NS:
                            shares(s + 1, a)
                        if s + 2 < NS:
                            scores_min(s + 2, a)
                for r in range(NS):
                    if CUM[r + 1] + 1 == k:
                        mixed_lo(r)
            mixed_lo(NS - 1)

            ln_chained = [0]

            def ln_chain(op):
                ln_chained[0] += 1
                op.then_inc(ln_step, 1)
                dve.wait_ge(ln_step, ln_chained[0])

            def ln_moments(st):
                for n in range(2):
                    op = dve.bn_stats(stats[:, st % 2, n, :], y[:, st, n * HALF:(n + 1) * HALF])
                ln_chain(op)
                dve.bn_aggr(mv[:, st % 2, :], stats[:, st % 2, :, :]).then_inc(ln_stats, 1)

            def ln_finish(n, st):
                dve.wait_ge(ln_std, n + 1)
                dve.wait_ge(ln_stats, n + 1)
                ln_chain(dve.reciprocal(std[:, st % 2, 1:2], std[:, st % 2, 0:1]))
                yt = y[:, st, :]
                ln_chain(dve.scalar_tensor_tensor(out=yt, in0=yt, scalar=mv[:, st % 2, 0:1],
                                                  in1=gb[:, 0, :], op0=ALU.subtract, op1=ALU.mult))
                dve.scalar_tensor_tensor(out=yt, in0=yt, scalar=std[:, st % 2, 1:2],
                                         in1=gb[:, 1, :], op0=ALU.mult, op1=ALU.add).then_inc(ln_done, 1)

            def x1_lo_part(st):
                for h in range(2):
                    q = 2 * st + h
                    part = (slice(None), slice(4 * h, 4 * h + 4), slice(st * P, (st + 1) * P))
                    dve.wait_ge(x1_hi, q + 1)
                    dve.tensor_tensor(act_lo[part], psB[:, q % 4, :].rearrange("p (k n) -> p k n", k=4),
                                      act_hi[part].bitcast(F32), ALU.subtract).then_inc(psb_drained, 1)

            for nh in range(2):
                for st in range(ST + (2 if nh else 0)):
                    if st < ST:
                        q = nh * ST + st
                        if nh == 0:
                            dve.wait_ge(res_loaded[st], 16)
                        dve.wait_ge(wo_done, q + 1)
                        yp = y[:, st, nh * HALF:(nh + 1) * HALF]
                        dve.scalar_tensor_tensor(out=yp, in0=yp, scalar=ALPHA, in1=psA[:, q % 4, :],
                                                 op0=ALU.mult, op1=ALU.add).then_inc(y_added, 1)
                        if nh == 1:
                            dve.wait_ge(y_added, q + 1)
                            ln_moments(st)
                    if nh == 1 and 1 <= st <= ST:
                        if st == 1:
                            dve.wait_ge(ln_rows, 32)
                        ln_finish(st - 1, st - 1)
                    if nh == 1 and st >= 2:
                        x1_lo_part(st - 2)

            def gated_unit(n_gu, par, ch):
                for n in range(2):
                    dve.wait_ge(silu_done, n_gu + n + 1)
                    if not (isinstance(n_gu, int) and n_gu == 0):
                        dve.wait_ge(hlo_done, n_gu + (n - 1))
                    dve.tensor_tensor(h_t[:, n, :], psA[:, 2 * n + 1, :], silu_t[:, n, :], ALU.mult)\
                       .then_inc(h_done, 1)
                for n in range(2):
                    cols = slice(n * HALF, (n + 1) * HALF)
                    dve.wait_ge(hhi_done, n_gu + n + 1)
                    dve.tensor_tensor(h_lo[:, par, ch, cols], h_t[:, n, :],
                                      h_hi[:, par, ch, cols].bitcast(F32), ALU.subtract).then_inc(hlo_done, 1)

            def add_down(n_dn, st, nh):
                q = 2 * st + nh
                dve.wait_ge(dn_done, n_dn + q + 1)
                yp = y[:, st, nh * HALF:(nh + 1) * HALF]
                dve.tensor_tensor(yp, yp, psB[:, q % 4, :], ALU.add).then_inc(psb_drained, 1)

            dve.wait_ge(x1_scaled, ST)
            gated_unit(0, 0, 0)
            gated_unit(2, 0, 1)
            with dve.Fori(0, (GROUPS - 1) // 2) as it:
                for j in range(2):
                    gated_unit(8 * it + (4 + 4 * j), (j + 1) % 2, 0)
                    for q in range(16):
                        add_down(32 * it + 16 * j, q // 2, q % 2)
                    gated_unit(8 * it + (4 + 4 * j + 2), (j + 1) % 2, 1)
            n_dn = 16 * (GROUPS - 1)
            dve.wait_ge(ln_rows, 64)
            for st in range(ST + 1):
                if st < ST:
                    for nh in range(2):
                        add_down(n_dn, st, nh)
                    dve.wait_ge(psb_drained, X_Q + n_dn + 2 * st + 2)
                    ln_moments(st)
                if st >= 1:
                    ln_finish(ST + st - 1, st - 1)

        @block.tensor
        def _(pe):
            def product(dst, w, v, first, last):
                pe.matmul(dst, w[0], v[0], start=first, stop=False)
                pe.matmul(dst, w[0], v[1], start=False, stop=False)
                return pe.matmul(dst, w[1], v[0], start=False, stop=last)

            def act_cols(k, cols):
                return act_hi[:, k, cols], act_lo[:, k, cols]

            pe.wait_ge(consts_ready, 2)
            for Q in range(X_Q):
                st, h = divmod(Q, 2)
                if h == 0:
                    pe.wait_ge(x_loaded[st % 4], 16 * (st // 4 + 1))
                if Q >= 4:
                    pe.wait_ge(q_lo, Q - 3)
                for k in range(4):
                    c = 4 * h + k
                    op = pe.transpose(psA[:, Q % 4, k * P:(k + 1) * P],
                                      x_tile[:, st % 4, c * P:(c + 1) * P], ident[:, :])
                op.then_inc(q_done, 1)

            def unit_w(slot):
                return [as_chunks(w[:, slot, :]) for w in (w_hi, w_lo)]

            def feature_major(dst, slot, n):
                w = unit_w(slot)
                for k in range(KC):
                    op = product(dst, (w[0][:, k, :], w[1][:, k, :]),
                                 act_cols(k, slice(n * HALF, (n + 1) * HALF)), k == 0, k == KC - 1)
                return op

            pe.wait_ge(q_lo, X_Q)
            with pe.Fori(0, 3) as i:
                for c in range(4):
                    pe.wait_ge(wlo_ready, 6 * i + (c + 1))
                    for n in range(2):
                        Q = 2 * c + n
                        pe.wait_ge(q_lo, 12 * i + (X_Q + Q - 3))
                        op = feature_major(psA[:, Q % 4, :], c % 3, n)
                        op.then_inc(q_done, 1)
                pe.wait_ge(wlo_ready, 6 * i + 6)
                for v in range(4):
                    pe.wait_ge(q_lo, 12 * i + (X_Q + 8 + v - 3))
                    for s2 in range(2):
                        st = 2 * v + s2
                        for k in range(KC):
                            slot = (4 + k // 4) % 3
                            w = [t[:, slot, (k % 4) * 256:(k % 4 + 1) * 256] for t in (w_hi, w_lo)]
                            op = product(psA[:, v, s2 * 256:(s2 + 1) * 256],
                                         act_cols(k, slice(st * P, (st + 1) * P)), w,
                                         k == 0, k == KC - 1)
                    op.then_inc(q_done, 1)

            bank_free = {4: (conv_act, 1), 5: (conv_act, 2), 6: (conv_act, 3), 7: (conv_act, 4),
                         8: (conv_act, 5), 9: (conv_act, 6), 10: (gate_step, 1), 11: (gate_step, 2),
                         12: (conv_dve, 1), 13: (conv_dve, 2)}
            for c in range(7):
                u = PROJ_UNITS + c
                pe.wait_ge(wlo_ready, u + 1)
                for n in range(2):
                    v = 2 * c + n
                    if v in bank_free:
                        pe.wait_ge(*bank_free[v])
                    feature_major(psB[:, v % 4, :], u % 3, n).then_inc(conv_done, 1)

            def scores(s, a):
                pr, h, g = STEPS[s]
                par, W = pr % 2, width(s)
                if h == 0 and g == 0 and a == 0:
                    pe.wait_ge(qkv_loaded[par], 16 * 7 * (pr // 2 + 1))
                if s == 0 and a == 0:
                    pe.wait_ge(consts_ready, 8)
                    pe.wait_ge(q_lo, X_Q + 3 * KIND_Q)
                t, i = 2 * s + a, 2 * g + a
                if t >= 2:
                    if t - 2 < 32:
                        pe.wait_ge(z_read_act, t - 1)
                    else:
                        pe.wait_ge(z_read_dve, t - 2 - 32 + 1)
                q = q_st[par][h][:, i * P:(i + 1) * P]
                masked = kind(s) != DIL
                for b, c0 in enumerate(range(0, W, HALF)):
                    n = min(HALF, W - c0)
                    last = c0 + n == W
                    z = psA[:, 2 * a + b, 0:n]
                    pe.matmul(z, q, kh_st[par][h][:, c0:c0 + n], start=True, stop=False)
                    op = pe.matmul(z, q, kl_st[par][h][:, c0:c0 + n], start=False,
                                   stop=not (masked and last))
                    if masked and last:
                        op = pe.matmul(psA[:, 2 * a + b, n - 256:n], ident_bf[:, :],
                                       masks[:, int(kind(s) == SB), a, :], start=False, stop=True)
                op.then_inc(z_ready, 1)

            def transposes(s, j):
                k = CUM[s] + j
                if k >= 2:
                    pe.wait_ge(pt_lo_done, k - 1)
                else:
                    pe.wait_ge(conv_ready, 2)
                for a in range(2):
                    if j == 0:
                        pe.wait_ge(probs_ready, 2 * s + a + 1)
                    for b in range(2):
                        kb = 2 * j + b
                        op = pe.transpose(psB[:, k % 2, b * 256 + a * P:b * 256 + (a + 1) * P],
                                          probs[:, s % 3, a, kb * P:(kb + 1) * P], ident[:, :])
                op.then_inc(pt_ready, 1)

            def values(s, j):
                pr, h, g = STEPS[s]
                k = CUM[s] + j
                if j == 0 and s >= 2:
                    pe.wait_ge(o_lo, s - 1)
                pe.wait_ge(pt_lo_done, k + 1)
                for b in range(2):
                    v = [v_t[pr % 2][:, part, 2 * j + b, h * HD:h * HD + P] for part in range(2)]
                    op = product(psB[:, 2 + s % 2, 0:256], v, (pt_hi[:, k % 3, b, :], pt_lo[:, k % 3, b, :]),
                                 j == 0 and b == 0, j == g and b == 1)
                op.then_inc(pv_done, 1)

            for s in range(2):
                for a in range(2):
                    scores(s, a)
            for k, (s, j) in enumerate(QUANTA):
                transposes(s, j)
                for a in range(2):
                    if s + 2 < NS and j == min(a, STEPS[s][2]):
                        scores(s + 2, a)
                if k >= 2:
                    values(*QUANTA[k - 2])
            values(*QUANTA[-2])
            values(*QUANTA[-1])

            pe.wait_ge(conv_split, 2)
            pe.wait_ge(o_lo, NS)
            pe.wait_ge(z_read_dve, 64)

            def x1_transposes(st):
                pe.wait_ge(ln_done, st + 1)
                for h in range(2):
                    q = 2 * st + h
                    if q >= 4:
                        pe.wait_ge(psb_drained, q - 3)
                    for k in range(4):
                        c = 4 * h + k
                        op = pe.transpose(psB[:, q % 4, k * P:(k + 1) * P], y[:, st, c * P:(c + 1) * P],
                                          ident[:, :])
                    op.then_inc(x1_t, 1)

            for nh in range(2):
                for st in range(ST):
                    if st < ST:
                        q = nh * ST + st
                        if q >= 4:
                            pe.wait_ge(y_added, q - 3)
                        for k in range(KC):
                            u = 4 * nh + k // 2
                            if st == 0 and k % 2 == 0:
                                pe.wait_ge(w3lo_ready, u + 1)
                            w = [t[:, u % 6, (k % 2) * HALF:(k % 2 + 1) * HALF] for t in (w3_hi, w3_lo)]
                            op = product(psA[:, q % 4, :], act_cols(k, slice(st * P, (st + 1) * P)), w,
                                         k == 0, k == KC - 1)
                        op.then_inc(wo_done, 1)
                    if nh == 1 and st >= 2:
                        x1_transposes(st - 2)

            def gate_up(u, slot, n_gu, halves=range(2)):
                pe.wait_ge(w3lo_ready, u + 2)
                for n in halves:
                    if not (isinstance(n_gu, int) and n_gu == 0):
                        pe.wait_ge(h_done, n_gu + (n - 1))
                    for m in range(2):
                        w = [as_chunks(t[:, slot + m, :]) for t in (w3_hi, w3_lo)]
                        for k in range(KC):
                            op = product(psA[:, 2 * n + m, :], (w[0][:, k, :], w[1][:, k, :]),
                                         act_cols(k, slice(n * HALF, (n + 1) * HALF)), k == 0, k == KC - 1)
                    op.then_inc(gu_done, 1)

            def down(u, slot, n_dn, par, n_h):
                pe.wait_ge(w3lo_ready, u + 2)
                pe.wait_ge(hlo_done, n_h)
                for q in range(16):
                    st, nh = divmod(q, 2)
                    pe.wait_ge(psb_drained, n_dn + (X_Q + q - 3))
                    for ch in range(2):
                        w = [t[:, slot + ch, nh * HALF:(nh + 1) * HALF] for t in (w3_hi, w3_lo)]
                        cols = slice(st * P, (st + 1) * P)
                        op = product(psB[:, q % 4, :], (h_hi[:, par, ch, cols], h_lo[:, par, ch, cols]), w,
                                     ch == 0, ch == 1)
                    op.then_inc(dn_done, 1)

            pe.wait_ge(psb_drained, X_Q // 2)
            pe.wait_ge(y_added, 2 * ST)
            gate_up(8, 2, 0, [0])
            for st in (ST - 2, ST - 1):
                x1_transposes(st)
            pe.wait_ge(psb_drained, X_Q)
            gate_up(8, 2, 0, [1])
            gate_up(10, 4, 2)
            with pe.Fori(0, (GROUPS - 1) // 2) as it:
                for j in range(2):
                    at = 12 + 6 * j
                    gate_up(12 * it + at, 0, 8 * it + (4 + 4 * j))
                    down(12 * it + (at + 2), 2, 32 * it + 16 * j, j % 2, 8 * it + (4 + 4 * j))
                    gate_up(12 * it + (at + 4), 4, 8 * it + (4 + 4 * j + 2))
            down(72, 0, 16 * (GROUPS - 1), 0, 4 * GROUPS)


_NAMES = ["x", "w_in", "f_bias", "conv_w", "w_out", "rel_bias", "ln1_g", "ln1_b", "w_gate", "w_up",
          "w_down", "ln2_g", "ln2_b"]


def kernel(**inputs):
    import numpy as _np
    import concourse.bacc as _bacc
    from concourse import mybir as _mybir
    from concourse.bass_utils import run_bass_kernel_spmd as _run

    nc = _bacc.Bacc("TRN2", target_bir_lowering=False, num_devices=1)
    arrays, args = {}, []
    for name in _NAMES:
        a = _np.ascontiguousarray(inputs[name])
        arrays[f"in_{name}"] = a
        args.append(nc.dram_tensor(f"in_{name}", a.shape, _mybir.dt.from_np(a.dtype),
                                   kind="ExternalInput").ap())
    args.append(nc.dram_tensor("out_x", (1, S, D), F32, kind="ExternalOutput").ap())
    layer(nc, *args)
    r = _run(nc, [arrays], core_ids=[0])
    return r.results[0]["out_x"]
```

```python
from contextlib import ExitStack

import concourse.bass as bass
import numpy as np
from concourse import mybir

F32 = mybir.dt.float32
F32R = mybir.dt.float32r
BF16 = mybir.dt.bfloat16
ACT = mybir.ActivationFunctionType
ALU = mybir.AluOpType

P = 128
S = 1024
D = 1024
KC = D // P
ST = S // P
HALF = 512
HD = 64
SCALE = HD ** -0.5
FF = 2816
FC = FF // P
GROUPS = FC // 2
LN_AWAY = [3, 5]
PAIRED = (GROUPS - 3) // 2
GATES = 4
GATE_LO = 32
W_KIND = 3 * 256
CONV0 = 3 * W_KIND
GATE0 = CONV0 + 3 * 256
ALPHA = 2.0 ** 0.25
EPS = 1e-5
MASKED = 1e30
BUCKETS, MAX_DIST = 32, 2048
SB, DIL, FOX = 0, 1, 2
VW = 192
TAB = 1279
TOEP = 1152


def bucket_starts():
    d = np.arange(S)
    exact = BUCKETS // 2
    nf = np.maximum(d, 1).astype(np.float32)
    large = exact + (np.log(nf / np.float32(exact)) / np.float32(np.log(MAX_DIST / exact))
                     * np.float32(BUCKETS - exact)).astype(np.int32)
    b = np.where(d < exact, d, np.minimum(large, BUCKETS - 1))
    return [(int(k), int(np.argmax(b == k))) for k in range(BUCKETS) if (b == k).any()]


def layer(nc, x, w_in, f_bias, conv_w, w_out, rel_bias, ln1_g, ln1_b, w_gate, w_up, w_down,
          ln2_g, ln2_b, out):
    x, out = x[0], out[0]
    w_in, w_out, w_gate, w_up, w_down = w_in[0], w_out[0], w_gate[0], w_up[0], w_down[0]

    qk_scr = nc.dram_tensor("qk_scr", [6, 2, P, 2, S], F32, kind="Internal").ap()
    v_scr = nc.dram_tensor("v_scr", [6, P, 2, ST, VW], F32, kind="Internal").ap()
    tab_scr = nc.dram_tensor("tab_scr", [4, TAB], F32, kind="Internal").ap()
    cum_scr = nc.dram_tensor("cum_scr", [4, S], F32, kind="Internal").ap()

    X_Q = 2 * ST
    KIND_Q = 12
    PROJ_UNITS = 6 * 3
    CONV_ORDER = [("b", 0), ("c", 0), ("b", 1), ("h", 0), ("f", 0), ("c", 1), ("h", 1)]
    CONV_COL = {"b": CONV0, "c": CONV0 + 256, "h": CONV0 + 512}
    STEPS = [(pr, h, g) for pr in range(6) for h in range(2) for g in (0, 2, 1, 3)]
    NS = len(STEPS)
    CUM = [0]
    for _, _, g in STEPS:
        CUM.append(CUM[-1] + g + 1)
    QUANTA = [(s, j) for s in range(NS) for j in range(STEPS[s][2] + 1)]
    TILES = [(s, a) for s in range(2, NS) for a in range(2)]

    def on_dve(s, a):
        return kind(s) == SB and STEPS[s][2] >= 2 and a == 1

    def finished(s, a, dve):
        return sum(on_dve(r, b) == dve for r in range(s + 1) for b in range(2) if (r, b) <= (s, a))

    def start(s, a):
        return CUM[s - 2] + min(a, STEPS[s - 2][2])

    def kind(s):
        return STEPS[s][0] // 2

    def width(s, a=1):
        return (2 * STEPS[s][2] + a + 1) * P

    persistent, early, attn, late = ExitStack(), ExitStack(), ExitStack(), ExitStack()
    with persistent:
        def sb(stack, name, shape, dt=F32):
            return stack.enter_context(nc.sbuf_tensor(name, shape, dt))

        def sem(name):
            return persistent.enter_context(nc.semaphore(name))

        act_hi = sb(persistent, "act_hi", [P, KC, S], F32R)
        act_lo = sb(persistent, "act_lo", [P, KC, S], F32R)
        ident = sb(persistent, "ident", [P, P])
        zeros = sb(persistent, "zeros", [P, P])
        ident_bf = sb(persistent, "ident_bf", [P, P], BF16)
        eps_t = sb(persistent, "eps_t", [P, 1])
        table_t = sb(persistent, "table_t", [P, 1])

        to_attn = ExitStack()
        q_st, kh_st, kl_st, v_t = [], [], [], []

        def stacks(stack, par):
            for lst, nm in ((q_st, "q_st"), (kh_st, "kh_st"), (kl_st, "kl_st")):
                lst.append([sb(stack, f"{nm}{par}{h}", [P, S], F32R) for h in range(2)])
            v_t.append(sb(stack, f"v_t{par}", [P, 2, ST, VW], F32R))

        stacks(to_attn, 0)
        conv_out = sb(to_attn, "conv_out", [P, 2, S])
        masks = sb(to_attn, "masks", [P, 2, 2, 256], BF16)

        raw = sb(early, "raw", [P, 3, D])
        w_hi = sb(early, "w_hi", [P, 3, D], F32R)
        w_lo = sb(early, "w_lo", [P, 3, D], F32R)
        stg = sb(early, "stg", [P, 4, 2, HALF], F32R)
        stg_v = sb(early, "stg_v", [P, 2, 2, 2, 2, VW], F32R)
        scratch = sb(early, "scratch", [P, 4, D])
        conv_u = sb(early, "conv_u", [P, S + 2])
        gate_f = sb(early, "gate_f", [GATES, S])
        gate_e = sb(early, "gate_e", [GATES, S])
        conv_wt = sb(early, "conv_wt", [P, 3, 2])
        rel_t = sb(early, "rel_t", [4, BUCKETS])
        fb_t = sb(early, "fb_t", [4, 1])
        x_tile = scratch
        conv_b, conv_y, conv_c = scratch[:, 0:2, :], scratch[:, 2, :], scratch[:, 3, :]
        early.close()

        probs = [sb(attn, f"probs{n}", [P, 2, S]) for n in range(2)] + [conv_out]
        rest = [sb(attn, f"rest{n}", [P, 2, S]) for n in range(2)]
        pt_hi = sb(attn, "pt_hi", [P, 3, 2, 256], F32R)
        pt_lo = sb(attn, "pt_lo", [P, 3, 2, 256], F32R)
        bias_t = sb(attn, "bias_t", [P, 2, TOEP])
        negmax = sb(attn, "negmax", [P, 8])
        den = sb(attn, "den", [P, 8])
        rden = sb(attn, "rden", [P, 8])
        stacks(attn, 1)
        attn.close()
        to_attn.close()

        raw3 = sb(late, "raw3", [P, 3, D])
        w3 = sb(late, "w3", [P, 6, 2, D], F32R)
        w3_hi, w3_lo = w3[:, :, 0, :], w3[:, :, 1, :]
        y = sb(late, "y", [P, ST, D])
        h_hi = sb(late, "h_hi", [P, 2, 2, S], F32R)
        h_lo = sb(late, "h_lo", [P, 2, 2, S], F32R)
        silu_t = sb(late, "silu_t", [P, 2, HALF])
        h_t = sb(late, "h_t", [P, 2, HALF])
        gb = sb(late, "gb", [P, 2, D])
        stats = sb(late, "stats", [P, 2, 2, 6])
        mv = sb(late, "mv", [P, 2, 2])
        std = sb(late, "std", [P, 2, 2])
        shift = sb(late, "shift", [P, 1])
        late.close()

        psA = persistent.enter_context(nc.psum_tensor("psA", [P, 4, HALF], F32))
        psB = persistent.enter_context(nc.psum_tensor("psB", [P, 4, HALF], F32))

        x_loaded = [sem(f"x_loaded{i}") for i in range(4)]
        small_loaded = sem("small_loaded")
        consts_ready = sem("consts_ready")
        raw_loaded = [sem(f"raw_loaded{i}") for i in range(3)]
        whi_ready, wlo_ready = sem("whi_ready"), sem("wlo_ready")
        q_done, q_hi, q_lo = sem("q_done"), sem("q_hi"), sem("q_lo")
        stored_qk = [sem(f"stored_qk{i}") for i in range(4)]
        stored_v = [sem(f"stored_v{i}") for i in range(2)]
        fixed_ready = sem("fixed_ready")
        tab_ready, tab_stored = sem("tab_ready"), sem("tab_stored")
        conv_done, conv_act, conv_dve = sem("conv_done"), sem("conv_act"), sem("conv_dve")
        conv_ready = sem("conv_ready")
        gate_step, gate_added = sem("gate_step"), sem("gate_added")
        cum_ready, cum_stored = sem("cum_ready"), sem("cum_stored")
        qkv_loaded = [sem("qkv_loaded0"), sem("qkv_loaded1")]
        bias_loaded = [sem("bias_loaded0"), sem("bias_loaded1")]
        z_ready, z_read_act, z_read_dve = sem("z_ready"), sem("z_read_act"), sem("z_read_dve")
        exp_done, rden_ready, probs_ready = sem("exp_done"), sem("rden_ready"), sem("probs_ready")
        probs_ready_dve = sem("probs_ready_dve")
        rest_scanned = sem("rest_scanned")
        pt_ready, pt_hi_done, pt_lo_done = sem("pt_ready"), sem("pt_hi_done"), sem("pt_lo_done")
        pv_done, o_hi, o_lo = sem("pv_done"), sem("o_hi"), sem("o_lo")
        conv_split = sem("conv_split")
        raw3_loaded = [sem(f"raw3_loaded{i}") for i in range(3)]
        w3hi_ready, w3lo_ready = sem("w3hi_ready"), sem("w3lo_ready")
        res_loaded, ln_rows = [sem(f"res_loaded{i}") for i in range(ST)], sem("ln_rows")
        wo_done, y_added = sem("wo_done"), sem("y_added")
        ln_stats, ln_std, ln_step, ln_done = sem("ln_stats"), sem("ln_std"), sem("ln_step"), sem("ln_done")
        x1_t, x1_hi, x1_scaled = sem("x1_t"), sem("x1_hi"), sem("x1_scaled")
        gu_done, silu_done, h_done = sem("gu_done"), sem("silu_done"), sem("h_done")
        hhi_done, hlo_done = sem("hhi_done"), sem("hlo_done")
        dn_done, psb_drained = sem("dn_done"), sem("psb_drained")
        ln_shift, ln_scaled = sem("ln_shift"), sem("ln_scaled")
        ln_times_g, ln_done_away = sem("ln_times_g"), sem("ln_done_away")
        stored = sem("stored")
        dve_step = sem("dve_step")

        def in_unit(col):
            return w_in[:, col].rearrange("(k p) n -> p k n", p=P)

        def as_chunks(slot):
            return slot.rearrange("p (k n) -> p k n", k=KC)

        def x_bank(Q):
            return (psA if Q < X_Q // 2 else psB)[:, Q % 4, :]

        def w3_unit(u):
            if u < 6:
                return w3_hi[:, u, :], w3_lo[:, u, :]
            return h_hi[:, 1, u - 6, :], h_lo[:, 1, u - 6, :]

        block = persistent.enter_context(nc.Block())

        @block.sync
        def _(sp):
            QK_COL = [0, 256, 128, 384]

            def load_qk(col, slot):
                sp.dma_start(as_chunks(raw[:, slot, :]), in_unit(col)).then_inc(raw_loaded[slot], 16)

            def load_v(kind_i, half, slot):
                rows = w_in[half * HALF:(half + 1) * HALF, bass.ds(kind_i * W_KIND + 512, 256)]
                sp.dma_start(raw[:, slot, :].rearrange("p (k n) -> p k n", k=4),
                             rows.rearrange("(k p) n -> p k n", p=P)).then_inc(raw_loaded[slot], 16)

            for st in range(ST):
                if st == 3:
                    load_qk(slice(QK_COL[0], QK_COL[0] + P), 0)
                if st >= 4:
                    sp.wait_ge(q_done, 2 * (st - 3))
                sp.dma_start(x_tile[:, st % 4, :], x[st * P:(st + 1) * P, :])\
                  .then_inc(x_loaded[st % 4], 16)
            sp.dma_start(rel_t[:, :], rel_bias.rearrange("b h -> h b"), allow_slow_non_contiguous=True)\
              .then_inc(small_loaded, 16)
            sp.dma_start(fb_t[:, :], f_bias.rearrange("a h -> h a"), allow_slow_non_contiguous=True)\
              .then_inc(small_loaded, 16)
            sp.dma_start(conv_wt[:, :, :], conv_w[0].rearrange("j (c p) -> p j c", p=P),
                         allow_slow_non_contiguous=True)\
              .then_inc(small_loaded, 16)
            for c in (1, 2):
                load_qk(slice(QK_COL[c], QK_COL[c] + P), c)
            sp.wait_ge(tab_ready, 1)
            sp.dma_start(tab_scr, conv_out[0:4].rearrange("p a n -> p (a n)")[:, 0:TAB])\
              .then_inc(tab_stored, 16)

            with sp.Fori(0, 3) as i:
                for c in range(6):
                    sp.wait_ge(whi_ready, 6 * i + (c + 1))
                    sp.wait_ge(wlo_ready, 6 * i + (c + 1))
                    if c == 0:
                        load_qk(bass.ds(i * W_KIND + QK_COL[3], P), 0)
                    elif c < 3:
                        load_v(i, c - 1, c)
                    else:
                        load_qk(bass.ds(i * W_KIND + (W_KIND + QK_COL[c - 3]), P), c - 3)
                    if c < 4:
                        for n in range(2):
                            sp.wait_ge(q_lo, 12 * i + (X_Q + 2 * c + n + 1))
                            slot = (2 * c + n) % 4
                            sp.dma_start(
                                qk_scr[bass.ds(2 * i + c // 2, 1), c % 2, :, :, n * HALF:(n + 1) * HALF]
                                .rearrange("a p t n -> (a p) t n"),
                                stg[:, slot, :, :].bitcast(F32)).then_inc(stored_qk[slot], 16)
                    elif c == 5:
                        for v in range(4):
                            sp.wait_ge(q_lo, 12 * i + (X_Q + 8 + v + 1))
                            for pr in range(2):
                                sp.dma_start(
                                    v_scr[bass.ds(2 * i + pr, 1), :, :, 2 * v:2 * v + 2, :]
                                    .rearrange("a p t s n -> (a p) t (s n)"),
                                    stg_v[:, v % 2, :, pr, :, :].rearrange("p t s n -> p t (s n)")
                                    .bitcast(F32))\
                                  .then_inc(stored_v[v % 2], 16)
            for c in range(3, 7):
                u = PROJ_UNITS + c
                sp.wait_ge(whi_ready, u - 2)
                sp.wait_ge(wlo_ready, u - 2)
                what, ch = CONV_ORDER[c]
                if what == "f":
                    dst = as_chunks(raw[:, u % 3, :])
                    sp.dma_start(dst[:, :, 0:GATES], in_unit(slice(GATE0, GATE0 + GATES)))\
                      .then_inc(raw_loaded[u % 3], 16)
                    sp.dma_start(dst[:, :, GATES:P], in_unit(slice(0, P - GATES)))\
                      .then_inc(raw_loaded[u % 3], 16)
                else:
                    col = CONV_COL[what] + ch * P
                    load_qk(slice(col, col + P), u % 3)

            for k in range(4):
                sp.wait_ge(stored_qk[k], 16 * 6)
            for k in range(2):
                sp.wait_ge(stored_v[k], 16 * 12)

            def load_pair(pr):
                par = pr % 2
                for h in range(2):
                    for which, part, stride, dst in ((0, 0, S, q_st), (1, 0, 0, kh_st), (1, 1, 0, kl_st)):
                        at = ((pr * 2 + which) * P + h * HD) * 2 * S + part * S
                        sp.dma_start(dst[par][h][:, :].bitcast(F32),
                                     bass.AP(qk_scr.tensor, at, [[stride, 2], [2 * S, HD], [1, S]]))\
                          .then_inc(qkv_loaded[par], 16)
                sp.dma_start(v_t[par][:, :, :, :].bitcast(F32), v_scr[pr]).then_inc(qkv_loaded[par], 16)

            def load_bias(hd):
                if hd < 8:
                    src = bass.AP(tab_scr.tensor, (hd - 4) * TAB, [[1, P], [1, TOEP]])
                    dst = bias_t[:, hd % 2, :]
                else:
                    src = bass.AP(cum_scr.tensor, (hd - 8) * S, [[0, P], [1, S]])
                    dst = bias_t[:, hd % 2, 0:S]
                sp.dma_start(dst, src).then_inc(bias_loaded[hd % 2], 16)

            load_pair(0)
            sp.wait_ge(tab_stored, 16)
            sp.wait_ge(cum_ready, 1)
            sp.dma_start(cum_scr, gate_e[:, :]).then_inc(cum_stored, 16)
            sp.wait_ge(cum_stored, 16)
            sp.wait_ge(conv_ready, 4)
            load_pair(1)
            load_bias(4)
            load_bias(5)
            for pr in range(2, 6):
                sp.wait_ge(pv_done, CUM[8 * (pr - 1)])
                load_pair(pr)
                for hd in (2 * pr, 2 * pr + 1) if pr > 2 else ():
                    sp.wait_ge(z_read_dve, 8 * (hd - 2 - 4) + 8)
                    load_bias(hd)

            sp.wait_ge(pv_done, CUM[8 * 5])

            def slot_free(u):
                if isinstance(u, int) and u < 3:
                    return
                sp.wait_ge(w3hi_ready, u - 2)
                sp.wait_ge(w3lo_ready, u - 2)

            for u in range(8):
                if u == 6:
                    sp.wait_ge(o_lo, NS)
                    sp.wait_ge(conv_split, 2)
                    for st in range(ST):
                        sp.dma_start(y[:, st, :], x[st * P:(st + 1) * P, :])\
                          .then_inc(res_loaded[st], 16)
                    for k, row in enumerate((ln1_g, ln1_b)):
                        sp.dma_start(gb[:, k, :], bass.AP(row.tensor, 0, [[0, P], [1, D]]))\
                          .then_inc(ln_rows, 16)
                slot_free(u)
                nh, kp = divmod(u, 4)
                src = w_out[2 * kp * P:(2 * kp + 2) * P, nh * HALF:(nh + 1) * HALF]
                sp.dma_start(raw3[:, u % 3, :].rearrange("p (k n) -> p k n", k=2),
                             src.rearrange("(k p) n -> p k n", p=P)).then_inc(raw3_loaded[u % 3], 16)

            def load_gu(u, slot, w, chunk):
                slot_free(u)
                sp.dma_start(as_chunks(raw3[:, slot, :]),
                             w[:, bass.ds(chunk * P, P)].rearrange("(k p) n -> p k n", p=P))\
                  .then_inc(raw3_loaded[slot], 16)

            def load_dn(u, slot, chunk):
                slot_free(u)
                sp.dma_start(raw3[:, slot, :], w_down[bass.ds(chunk * P, P), :])\
                  .then_inc(raw3_loaded[slot], 16)

            for c in range(2):
                load_gu(8 + 2 * c, (8 + 2 * c) % 3, w_gate, c)
                load_gu(9 + 2 * c, (9 + 2 * c) % 3, w_up, c)

            def load_group(it, j):
                at = 12 + 6 * j
                load_gu(12 * it + at, at % 3, w_gate, 4 * it + (2 * j + 2))
                load_gu(12 * it + (at + 1), (at + 1) % 3, w_up, 4 * it + (2 * j + 2))
                load_dn(12 * it + (at + 2), (at + 2) % 3, 4 * it + 2 * j)
                load_dn(12 * it + (at + 3), (at + 3) % 3, 4 * it + (2 * j + 1))
                load_gu(12 * it + (at + 4), (at + 4) % 3, w_gate, 4 * it + (2 * j + 3))
                load_gu(12 * it + (at + 5), (at + 5) % 3, w_up, 4 * it + (2 * j + 3))

            with sp.Fori(0, PAIRED) as it:
                for j in range(2):
                    load_group(it, j)
            load_group(PAIRED, 0)
            for c in range(2):
                load_gu(66 + 2 * c, (66 + 2 * c) % 3, w_gate, FC - 2 + c)
                load_gu(67 + 2 * c, (67 + 2 * c) % 3, w_up, FC - 2 + c)
            for c in range(4):
                load_dn(70 + c, (70 + c) % 3, FC - 4 + c)
            sp.wait_ge(ln_done, ST)
            for k, row in enumerate((ln2_g, ln2_b)):
                sp.dma_start(gb[:, k, :], bass.AP(row.tensor, 0, [[0, P], [1, D]]))\
                  .then_inc(ln_rows, 16)
            for st in range(ST - 1):
                away = sum(r < st for r in LN_AWAY)
                if st in LN_AWAY:
                    sp.wait_ge(ln_done_away, away + 1)
                else:
                    sp.wait_ge(ln_done, ST + st + 1 - away)
                sp.dma_start(out[st * P:(st + 1) * P, :], y[:, st, :]).then_inc(stored, 16)
            for nh in range(2):
                cols = slice(nh * HALF, (nh + 1) * HALF)
                sp.wait_ge(ln_done, 2 * ST + nh - len(LN_AWAY))
                sp.dma_start(out[S - P:S, cols], y[:, ST - 1, cols]).then_inc(stored, 16)
            sp.wait_ge(stored, 16 * (ST + 1))

        @block.gpsimd
        def _(pool):
            pool.memset(ident[:, :], 0.0).then_inc(consts_ready, 1)
            pool.wait_ge(consts_ready, 1)
            pool.affine_select(out=ident[:, :], in_=ident[:, :], compare_op=ALU.not_equal, fill=1.0,
                               base=0, pattern=[[-1, P]], channel_multiplier=1).then_inc(consts_ready, 1)
            pool.memset(stg_v[:, :, :, :, :, HD:P].rearrange("p s t r k n -> p (s t r k) n").bitcast(F32),
                        0.0).then_inc(fixed_ready, 1)
            pool.memset(zeros[:, :], 0.0).then_inc(fixed_ready, 1)
            pool.memset(conv_u[:, 0:2], 0.0).then_inc(fixed_ready, 1)
            pool.memset(eps_t[:, :], EPS).then_inc(fixed_ready, 1)
            pool.wait_ge(consts_ready, 2)
            pool.tensor_copy(ident_bf[:, :], ident[:, :]).then_inc(consts_ready, 1)
            pool.memset(masks[:, :, :, :].rearrange("p a b n -> p (a b n)"), 0.0).then_inc(consts_ready, 1)
            pool.wait_ge(consts_ready, 4)
            for strict in range(2):
                for a in range(2):
                    m = masks[:, strict, a, :]
                    pool.affine_select(out=m, in_=m, compare_op=ALU.is_gt if strict else ALU.is_ge,
                                       fill=MASKED, base=a * P, pattern=[[-1, 256]],
                                       channel_multiplier=1).then_inc(consts_ready, 1)

            def split_lo(u, slot, n_loaded):
                pool.wait_ge(raw_loaded[slot], n_loaded)
                pool.wait_ge(whi_ready, u + 1)
                pool.tensor_tensor(w_lo[:, slot, :], raw[:, slot, :], w_hi[:, slot, :].bitcast(F32),
                                   ALU.subtract).then_inc(wlo_ready, 1)

            with pool.Fori(0, 3) as i:
                for c in range(6):
                    split_lo(6 * i + c, c % 3, 32 * i + 16 * (c // 3 + 1))
            for c in range(7):
                u = PROJ_UNITS + c
                if CONV_ORDER[c][0] != "f":
                    split_lo(u, u % 3, 16 * (u // 3 + 1))
                else:
                    hi = as_chunks(w_hi[:, u % 3, :])
                    pool.wait_ge(raw_loaded[u % 3], 16 * (u // 3 + 2))
                    pool.wait_ge(whi_ready, u + 1)
                    pool.tensor_tensor(hi[:, :, GATE_LO:GATE_LO + GATES],
                                       as_chunks(raw[:, u % 3, :])[:, :, 0:GATES],
                                       hi[:, :, 0:GATES].bitcast(F32), ALU.subtract).then_inc(wlo_ready, 1)

            def probabilities(s, a):
                t, W = 2 * s + a, width(s, a)
                p = probs[s % 3][:, a, 0:W]
                if kind(s) == SB:
                    pool.wait_ge(rest_scanned, t + 1)
                    pool.tensor_tensor(p[:, 0:W - 1], p[:, 0:W - 1], rest[s % 2][:, a, 1:W], ALU.mult)\
                        .then_inc(probs_ready, 1)
                else:
                    pool.wait_ge(rden_ready, t - 32 + 1)
                    pool.tensor_tensor(p, p, rden[:, t % 8:t % 8 + 1].broadcast_to([P, W]), ALU.mult)\
                        .then_inc(probs_ready, 1)

            def split3_lo(u, slot, n_loaded):
                pool.wait_ge(raw3_loaded[slot % 3], n_loaded)
                pool.wait_ge(w3hi_ready, u + 1)
                pool.tensor_tensor(w3_lo[:, slot, :], raw3[:, slot % 3, :], w3_hi[:, slot, :].bitcast(F32),
                                   ALU.subtract).then_inc(w3lo_ready, 1)

            for s in range(NS):
                for a in range(2):
                    if not on_dve(s, a):
                        probabilities(s, a)

            for u in range(12):
                if u in (6, 7):
                    hi, lo = w3_unit(u)
                    pool.wait_ge(raw3_loaded[u % 3], 16 * (u // 3 + 1))
                    pool.wait_ge(w3hi_ready, u + 1)
                    pool.tensor_tensor(lo, raw3[:, u % 3, :], hi.bitcast(F32), ALU.subtract)\
                        .then_inc(w3lo_ready, 1)
                else:
                    split3_lo(u, u % 6, 16 * (u // 3 + 1))
            with pool.Fori(0, PAIRED) as it:
                for c in range(12):
                    split3_lo(12 * it + (12 + c), c % 6, 64 * it + 16 * (4 + c // 3 + 1))
            for u in range(12 + 12 * PAIRED, 8 + 3 * FC):
                split3_lo(u, u % 6, 16 * (u // 3 + 1))
            pool.wait_ge(ln_rows, 64)
            for n, st in enumerate(LN_AWAY):
                pool.wait_ge(ln_scaled, n + 1)
                pool.tensor_tensor(y[:, st, :], y[:, st, :], gb[:, 0, :], ALU.mult).then_inc(ln_times_g, 1)
                pool.wait_ge(ln_times_g, n + 1)
                pool.tensor_tensor(y[:, st, :], y[:, st, :], gb[:, 1, :], ALU.add).then_inc(ln_done_away, 1)

        @block.scalar
        def _(act):
            def split_hi(slot, n_loaded):
                act.wait_ge(raw_loaded[slot], n_loaded)
                act.activation(w_hi[:, slot, :], raw[:, slot, :], ACT.Copy).then_inc(whi_ready, 1)

            for Q in range(X_Q):
                st, h = divmod(Q, 2)
                if Q == 5:
                    split_hi(0, 16)
                act.wait_ge(q_done, Q + 1)
                act.activation(act_hi[:, 4 * h:4 * h + 4, st * P:(st + 1) * P],
                               x_bank(Q).rearrange("p (k n) -> p k n", k=4), ACT.Copy)\
                   .then_inc(q_hi, 1)

            for c in (1, 2):
                split_hi(c, 16)
            act.wait_ge(fixed_ready, 1)
            with act.Fori(0, 3) as i:
                for c in range(6):
                    if c < 4:
                        for n in range(2):
                            Q = 2 * c + n
                            act.wait_ge(q_done, 12 * i + (X_Q + Q + 1))
                            if Q >= 4:
                                act.wait_ge(stored_qk[Q % 4], 32 * i + 16)
                            act.activation(stg[:, Q % 4, 0, :], psA[:, Q % 4, :], ACT.Copy,
                                           scale=-SCALE if c % 2 == 0 else 1.0).then_inc(q_hi, 1)
                    elif c == 5:
                        for v in range(4):
                            act.wait_ge(q_done, 12 * i + (X_Q + 8 + v + 1))
                            if v >= 2:
                                act.wait_ge(stored_v[v % 2], 64 * i + 32)
                            for pr in range(2):
                                op = act.activation(
                                    stg_v[:, v % 2, 0, pr, :, :]
                                    .rearrange("p s (w n) -> p s w n", n=HD)[:, :, 0:3:2, :],
                                    psA[:, v, :].rearrange("p (s r w n) -> p s r w n", s=2, r=2, w=2)
                                    [:, :, pr, :, :], ACT.Copy)
                            op.then_inc(q_hi, 1)
                    for d in {4: (), 5: (4, 5)}.get(c, (c,)):
                        split_hi(d % 3, 32 * i + 16 * ((d + 3) // 3 + 1))
                for k in range(4):
                    act.wait_ge(stored_qk[k], 32 * i + 32)
                for k in range(2):
                    act.wait_ge(stored_v[k], 64 * i + 64)

            act.wait_ge(tab_ready, 1)
            for c, (what, ch) in enumerate(CONV_ORDER):
                for n in range(2):
                    if what == "h":
                        continue
                    cols, bank = slice(n * HALF, (n + 1) * HALF), psB[:, (2 * c + n) % 4, :]
                    if c == 0 and n == 0:
                        act.wait_ge(q_done, X_Q + 3 * KIND_Q + 1)
                        bank = psA[:, 0, :]
                    else:
                        act.wait_ge(conv_done, 2 * c + n)
                    if what == "f":
                        act.activation(gate_f[:, cols], bank[0:GATES], ACT.Identity, bias=fb_t[:, 0:1])
                        act.activation(gate_e[:, cols], bank[GATE_LO:GATE_LO + GATES], ACT.Copy)\
                           .then_inc(gate_step, 1)
                        continue
                    if (what, ch, n) == ("c", 1, 0):
                        act.wait_ge(conv_dve, 2)
                    act.activation(conv_b[:, ch, cols] if what == "b" else conv_c[:, cols], bank,
                                   ACT.Copy).then_inc(conv_act, 1)
                if what == "f":
                    act.wait_ge(gate_added, 1)
                    act.activation(gate_e[:, :], gate_f[:, :], ACT.Abs).then_inc(gate_step, 1)
                    act.wait_ge(gate_step, 3)
                    act.activation(gate_e[:, :], gate_e[:, :], ACT.Exp, scale=-1.0).then_inc(gate_step, 1)
                    act.wait_ge(gate_step, 4)
                    act.activation(gate_e[:, :], gate_e[:, :], ACT.Ln, bias=1.0).then_inc(gate_step, 1)
                if c + 3 < len(CONV_ORDER):
                    u = PROJ_UNITS + c + 3
                    act.wait_ge(conv_done, 2 * c + 1)
                    split_hi(u % 3, 16 * (u // 3 + 1) + 16 * (c + 3 == 4))

            act.wait_ge(fixed_ready, 4)
            act.activation(table_t[:, :], eps_t[:, :], ACT.Sigmoid)

            def softmax_part(s, a):
                t, W = 2 * s + a, width(s, a)
                p = probs[s % 3][:, a, 0:W]
                if kind(s) == SB:
                    z = psA[:, 2 * a:2 * a + 2, :].rearrange("p b n -> p (b n)")[:, 0:W]
                    if s >= 3:
                        act.wait_ge(pt_ready, CUM[s - 2])
                    elif s == 2:
                        act.wait_ge(conv_split, 2)
                    act.wait_ge(z_ready, t + 1)
                    act.activation(p, z, ACT.Sigmoid, scale=-1.0)
                    if s >= 2:
                        if on_dve(s - 2, a):
                            act.wait_ge(probs_ready_dve, finished(s - 2, a, True))
                        else:
                            act.wait_ge(probs_ready, finished(s - 2, a, False))
                    act.activation(rest[s % 2][:, a, 0:W], z, ACT.Sigmoid).then_inc(z_read_act, 1)
                else:
                    act.wait_ge(z_read_dve, t - 32 + 1)
                    act.activation(p, p, ACT.Exp, bias=negmax[:, t % 8:t % 8 + 1], scale=-1.0,
                                   accum_out=den[:, t % 8:t % 8 + 1]).then_inc(exp_done, 1)

            def transposed_hi(s, j):
                k = CUM[s] + j
                act.wait_ge(pt_ready, k + 1)
                if k >= 3:
                    act.wait_ge(pv_done, k - 2)
                act.activation(pt_hi[:, k % 3, :, :].rearrange("p b n -> p (b n)"), psB[:, k % 2, :],
                               ACT.Copy).then_inc(pt_hi_done, 1)

            def mixed_hi(s):
                pr, h, g = STEPS[s]
                act.wait_ge(pv_done, CUM[s + 1])
                lanes = slice(h * HD, (h + 1) * HD)
                act.activation(act_hi[lanes, pr, g * 256:(g + 1) * 256], psB[lanes, 2 + s % 2, 0:256],
                               ACT.Copy).then_inc(o_hi, 1)

            def split3_hi(slot, n_loaded):
                act.wait_ge(raw3_loaded[slot % 3], n_loaded)
                act.activation(w3_hi[:, slot, :], raw3[:, slot % 3, :], ACT.Copy).then_inc(w3hi_ready, 1)

            for s in range(2):
                for a in range(2):
                    softmax_part(s, a)
                act.wait_ge(conv_ready, 2 * s + 2)
                act.activation(act_hi[:, 6 + s, :], conv_out[:, s, :], ACT.Copy).then_inc(q_hi, 1)
            for k, (s, j) in enumerate(QUANTA):
                transposed_hi(s, j)
                for r, a in TILES:
                    if start(r, a) + (0 if kind(r) == SB else 1) == k:
                        softmax_part(r, a)
                for r in range(NS):
                    if CUM[r + 1] + 1 == k:
                        mixed_hi(r)
                if CUM[NS - 2] <= k < CUM[NS - 2] + 3:
                    split3_hi(k - CUM[NS - 2], 16)
            mixed_hi(NS - 1)

            def split3(u):
                if u in (6, 7):
                    act.wait_ge(raw3_loaded[u % 3], 16 * (u // 3 + 1))
                    act.activation(w3_unit(u)[0], raw3[:, u % 3, :], ACT.Copy).then_inc(w3hi_ready, 1)
                    return
                if u >= 8:
                    act.wait_ge(wo_done, ST if u < 10 else 2 * ST)
                split3_hi(u % 6, 16 * (u // 3 + 1))

            def ln_root(n, st):
                act.wait_ge(ln_stats, n + 1)
                act.activation(std[:, st % 2, 0:1], mv[:, st % 2, 1:2], ACT.Sqrt, bias=eps_t[:, 0:1])\
                   .then_inc(ln_std, 1)

            def x1_hi_part(st):
                for h in range(2):
                    q = 2 * st + h
                    act.wait_ge(x1_t, q + 1)
                    act.activation(act_hi[:, 4 * h:4 * h + 4, st * P:(st + 1) * P],
                                   psB[:, q % 4, :].rearrange("p (k n) -> p k n", k=4), ACT.Copy)\
                       .then_inc(x1_hi, 1)
                act.activation(y[:, st, :], y[:, st, :], ACT.Copy, scale=ALPHA).then_inc(x1_scaled, 1)

            for u in range(3, 10):
                split3(u)
            for st in range(ST + 2):
                if st < ST:
                    ln_root(st, st)
                if st >= 2:
                    x1_hi_part(st - 2)
            for u in range(10, 14):
                split3(u)

            def gated_unit(n_gu, par, ch):
                for n in range(2):
                    act.wait_ge(gu_done, n_gu + n + 1)
                    act.activation(silu_t[:, n, :], psA[:, 2 * n, :], ACT.Silu).then_inc(silu_done, 1)
                for n in range(2):
                    act.wait_ge(h_done, n_gu + n + 1)
                    act.activation(h_hi[:, par, ch, n * HALF:(n + 1) * HALF], h_t[:, n, :], ACT.Copy)\
                       .then_inc(hhi_done, 1)

            gated_unit(0, 0, 0)
            gated_unit(2, 0, 1)

            def group(it, j):
                for m in range(3):
                    for c in range(2):
                        u = 12 + 6 * j + 2 * m + 2 + c
                        split3_hi(u % 6, 64 * it + 16 * (u // 3 + 1))
                    if m != 1:
                        gated_unit(8 * it + (4 + 4 * j + m), (j + 1) % 2, m // 2)

            with act.Fori(0, PAIRED) as it:
                for j in range(2):
                    group(it, j)
            group(PAIRED, 0)
            for c in range(2):
                for u in ((68, 69), (70, 71, 72, 73))[c]:
                    split3_hi(u % 6, 16 * (u // 3 + 1))
                gated_unit(4 * (GROUPS - 1) + 2 * c, 0, c)
            for st in range(ST):
                if st - 1 in LN_AWAY:
                    act.wait_ge(ln_shift, LN_AWAY.index(st - 1) + 1)
                    act.activation(y[:, st - 1, :], y[:, st - 1, :], ACT.Identity, bias=shift[:, 0:1],
                                   scale=std[:, (st - 1) % 2, 1:2]).then_inc(ln_scaled, 1)
                ln_root(ST + st, st)

        @block.vector
        def _(dve):
            chained = [0]

            def chain(op):
                chained[0] += 1
                op.then_inc(dve_step, 1)
                dve.wait_ge(dve_step, chained[0])

            for Q in range(X_Q):
                st, h = divmod(Q, 2)
                part = (slice(None), slice(4 * h, 4 * h + 4), slice(st * P, (st + 1) * P))
                dve.wait_ge(q_hi, Q + 1)
                dve.tensor_tensor(act_lo[part], x_bank(Q).rearrange("p (k n) -> p k n", k=4),
                                  act_hi[part].bitcast(F32), ALU.subtract).then_inc(q_lo, 1)

            tab = conv_out[0:4].rearrange("p a n -> p (a n)")[:, 0:TAB]
            base = conv_u[0:4, 2:2 + S]
            dve.wait_ge(small_loaded, 48)
            chain(dve.memset(base, 0.0))
            chain(dve.memset(tab, MASKED))
            starts = bucket_starts()
            for n, (b, d0) in enumerate(starts):
                d1 = starts[n + 1][1] if n + 1 < len(starts) else S
                seg = base[:, d0:d1]
                op = dve.scalar_tensor_tensor(out=seg, in0=seg, scalar=rel_t[:, b:b + 1], in1=seg,
                                              op0=ALU.subtract, op1=ALU.add)
            chain(op)
            for lo, hi, step, count in ((0, 128, 1, 1), (0, 128, 4, 2), (0, 128, 16, 3),
                                        (132, 512, 4, 1), (144, 512, 16, 2), (528, 1008, 16, 1)):
                chain(dve.tensor_scalar(tab[:, lo + TAB - S:hi + 1 + TAB - S:step], base[:, lo:hi + 1:step],
                                        -float(np.log(count)), None, ALU.add))
            dve.memset(base, 0.0).then_inc(tab_ready, 1)

            dve.wait_ge(fixed_ready, 1)
            with dve.Fori(0, 3) as i:
                for c in range(4):
                    for n in range(2):
                        Q = 2 * c + n
                        dve.wait_ge(q_hi, 12 * i + (X_Q + Q + 1))
                        if c % 2 == 0:
                            op = dve.scalar_tensor_tensor(
                                out=stg[:, Q % 4, 1, :], in0=psA[:, Q % 4, :], scalar=-SCALE,
                                in1=stg[:, Q % 4, 0, :].bitcast(F32), op0=ALU.mult, op1=ALU.subtract)
                        else:
                            op = dve.tensor_tensor(stg[:, Q % 4, 1, :], psA[:, Q % 4, :],
                                                   stg[:, Q % 4, 0, :].bitcast(F32), ALU.subtract)
                        op.then_inc(q_lo, 1)
                for v in range(4):
                    dve.wait_ge(q_hi, 12 * i + (X_Q + 8 + v + 1))
                    for pr in range(2):
                        heads = [stg_v[:, v % 2, part, pr, :, :]
                                 .rearrange("p s (w n) -> p s w n", n=HD)[:, :, 0:3:2, :]
                                 for part in range(2)]
                        op = dve.tensor_tensor(
                            heads[1], psA[:, v, :].rearrange("p (s r w n) -> p s r w n", s=2, r=2, w=2)
                            [:, :, pr, :, :], heads[0].bitcast(F32), ALU.subtract)
                    op.then_inc(q_lo, 1)

            dve.wait_ge(tab_stored, 16)
            dve.wait_ge(fixed_ready, 4)
            n_act = {("c", 0): 2, ("c", 1): 6}
            for c, (what, ch) in enumerate(CONV_ORDER):
                if what == "f":
                    dve.wait_ge(gate_step, 2)
                    dve.tensor_tensor(gate_f[:, :], gate_f[:, :], gate_e[:, :], ALU.add)\
                       .then_inc(gate_added, 1)
                    dve.wait_ge(gate_step, 5)
                    chain(dve.scalar_tensor_tensor(out=gate_f[:, :], in0=gate_f[:, :], scalar=0.0,
                                                   in1=gate_e[:, :], op0=ALU.min, op1=ALU.subtract))
                    dve.tensor_tensor_scan(gate_e[:, :], gate_f[:, :], gate_f[:, :], 0.0, ALU.add,
                                           ALU.bypass).then_inc(cum_ready, 1)
                if what != "h":
                    continue
                for n in range(2):
                    dve.wait_ge(conv_done, 2 * c + n)
                    dve.wait_ge(conv_act, n_act["c", ch] + n + 1)
                    cols = slice(n * HALF, (n + 1) * HALF)
                    dve.tensor_tensor(conv_u[:, 2 + n * HALF:2 + (n + 1) * HALF],
                                      psB[:, (2 * c + n) % 4, :], conv_c[:, cols], ALU.mult)\
                       .then_inc(conv_dve, 1)
                    dve.wait_ge(conv_dve, 2 * ch + n + 1)
                    u_at = [slice(n * HALF + tap, (n + 1) * HALF + tap) for tap in range(3)]
                    chain(dve.tensor_scalar(conv_y[:, cols], conv_u[:, u_at[2]], conv_wt[:, 2, ch:ch + 1],
                                            None, ALU.mult))
                    for tap in (1, 0):
                        chain(dve.scalar_tensor_tensor(out=conv_y[:, cols], in0=conv_u[:, u_at[tap]],
                                                       scalar=conv_wt[:, tap, ch:ch + 1],
                                                       in1=conv_y[:, cols], op0=ALU.mult, op1=ALU.add))
                    dve.tensor_tensor(conv_out[:, ch, cols], conv_y[:, cols], conv_b[:, ch, cols], ALU.mult)\
                       .then_inc(conv_ready, 1)

            def scores_min(s, a):
                if kind(s) == SB:
                    return
                pr, h, g = STEPS[s]
                t, W, i = 2 * s + a, width(s, a), 2 * g + a
                hd = 2 * pr + h
                z = psA[:, 2 * a:2 * a + 2, :].rearrange("p b n -> p (b n)")[:, 0:W]
                if kind(s) == DIL:
                    end = TOEP - (896 - i * P)
                    bias = bias_t[:, h, end - W:end][:, ::-1]
                else:
                    bias = bias_t[:, h, 0:W]
                dve.wait_ge(z_ready, t + 1)
                dve.wait_ge(pt_ready, CUM[s - 2])
                if g == 0 and a == 0:
                    dve.wait_ge(bias_loaded[hd % 2], 16 * ((hd - 4) // 2 + 1))
                dve.tensor_tensor_reduce(out=probs[s % 3][:, a, 0:W], in0=z,
                                         in1=bias, scale=1.0, scalar=2 * MASKED,
                                         op0=ALU.add, op1=ALU.min,
                                         accum_out=negmax[:, t % 8:t % 8 + 1]).then_inc(z_read_dve, 1)

            def shares(s, a):
                t, W = 2 * s + a, width(s, a)
                if kind(s) == SB:
                    r = rest[s % 2][:, a, 0:W]
                    dve.wait_ge(z_read_act, t + 1)
                    dve.tensor_tensor_scan(r[:, ::-1], r[:, ::-1], r[:, ::-1], 1.0, ALU.mult, ALU.bypass)\
                       .then_inc(rest_scanned, 1)
                    if on_dve(s, a):
                        p = probs[s % 3][:, a, 0:W - 1]
                        dve.wait_ge(rest_scanned, t + 1)
                        dve.tensor_tensor(p, p, r[:, 1:W], ALU.mult).then_inc(probs_ready_dve, 1)
                else:
                    c = slice(t % 8, t % 8 + 1)
                    dve.wait_ge(exp_done, t - 32 + 1)
                    dve.reciprocal(rden[:, c], den[:, c]).then_inc(rden_ready, 1)

            def transposed_lo(s, j):
                k = CUM[s] + j
                dve.wait_ge(pt_hi_done, k + 1)
                dve.tensor_tensor(pt_lo[:, k % 3, :, :].rearrange("p b n -> p (b n)"), psB[:, k % 2, :],
                                  pt_hi[:, k % 3, :, :].rearrange("p b n -> p (b n)").bitcast(F32),
                                  ALU.subtract).then_inc(pt_lo_done, 1)

            def mixed_lo(s):
                pr, h, g = STEPS[s]
                dve.wait_ge(o_hi, s + 1)
                lanes = slice(h * HD, (h + 1) * HD)
                dve.tensor_tensor(act_lo[lanes, pr, g * 256:(g + 1) * 256], psB[lanes, 2 + s % 2, 0:256],
                                  act_hi[lanes, pr, g * 256:(g + 1) * 256].bitcast(F32), ALU.subtract)\
                   .then_inc(o_lo, 1)

            for s in range(2):
                for a in range(2):
                    shares(s, a)
                dve.wait_ge(q_hi, X_Q + 3 * KIND_Q + s + 1)
                dve.tensor_tensor(act_lo[:, 6 + s, :], conv_out[:, s, :],
                                  act_hi[:, 6 + s, :].bitcast(F32), ALU.subtract).then_inc(conv_split, 1)
            for k, (s, j) in enumerate(QUANTA):
                transposed_lo(s, j)
                for r, a in TILES:
                    if start(r, a) == k:
                        scores_min(r, a)
                for r, a in TILES:
                    if start(r, a) + 1 == k:
                        shares(r, a)
                for r in range(NS):
                    if CUM[r + 1] + 1 == k:
                        mixed_lo(r)
            mixed_lo(NS - 1)

            ln_chained = [0]

            def ln_chain(op):
                ln_chained[0] += 1
                op.then_inc(ln_step, 1)
                dve.wait_ge(ln_step, ln_chained[0])

            def ln_moments(st):
                for n in range(2):
                    op = dve.bn_stats(stats[:, st % 2, n, :], y[:, st, n * HALF:(n + 1) * HALF])
                ln_chain(op)
                dve.bn_aggr(mv[:, st % 2, :], stats[:, st % 2, :, :]).then_inc(ln_stats, 1)

            def ln_finish(n, st, parts=1):
                dve.wait_ge(ln_std, n + 1)
                dve.wait_ge(ln_stats, n + 1)
                ln_chain(dve.reciprocal(std[:, st % 2, 1:2], std[:, st % 2, 0:1]))
                yt = y[:, st, :]
                ln_chain(dve.scalar_tensor_tensor(out=yt, in0=yt, scalar=mv[:, st % 2, 0:1],
                                                  in1=gb[:, 0, :], op0=ALU.subtract, op1=ALU.mult))
                for part in range(parts):
                    cols = slice(part * D // parts, (part + 1) * D // parts)
                    dve.scalar_tensor_tensor(out=yt[:, cols], in0=yt[:, cols], scalar=std[:, st % 2, 1:2],
                                             in1=gb[:, 1, cols], op0=ALU.mult, op1=ALU.add)\
                       .then_inc(ln_done, 1)

            def x1_lo_part(st):
                for h in range(2):
                    q = 2 * st + h
                    part = (slice(None), slice(4 * h, 4 * h + 4), slice(st * P, (st + 1) * P))
                    dve.wait_ge(x1_hi, q + 1)
                    dve.tensor_tensor(act_lo[part], psB[:, q % 4, :].rearrange("p (k n) -> p k n", k=4),
                                      act_hi[part].bitcast(F32), ALU.subtract).then_inc(psb_drained, 1)

            for nh in range(2):
                for st in range(ST + (2 if nh else 0)):
                    if st < ST:
                        q = nh * ST + st
                        if nh == 0:
                            dve.wait_ge(res_loaded[st], 16)
                        dve.wait_ge(wo_done, q + 1)
                        yp = y[:, st, nh * HALF:(nh + 1) * HALF]
                        dve.scalar_tensor_tensor(out=yp, in0=yp, scalar=ALPHA, in1=psA[:, q % 4, :],
                                                 op0=ALU.mult, op1=ALU.add).then_inc(y_added, 1)
                        if nh == 1:
                            dve.wait_ge(y_added, q + 1)
                            ln_moments(st)
                    if nh == 1 and 1 <= st <= ST:
                        if st == 1:
                            dve.wait_ge(ln_rows, 32)
                        ln_finish(st - 1, st - 1)
                    if nh == 1 and st >= 2:
                        x1_lo_part(st - 2)

            def gated_unit(n_gu, par, ch):
                for n in range(2):
                    dve.wait_ge(silu_done, n_gu + n + 1)
                    if not (isinstance(n_gu, int) and n_gu == 0):
                        dve.wait_ge(hlo_done, n_gu + (n - 1))
                    dve.tensor_tensor(h_t[:, n, :], psA[:, 2 * n + 1, :], silu_t[:, n, :], ALU.mult)\
                       .then_inc(h_done, 1)
                for n in range(2):
                    cols = slice(n * HALF, (n + 1) * HALF)
                    dve.wait_ge(hhi_done, n_gu + n + 1)
                    dve.tensor_tensor(h_lo[:, par, ch, cols], h_t[:, n, :],
                                      h_hi[:, par, ch, cols].bitcast(F32), ALU.subtract).then_inc(hlo_done, 1)

            def add_down(n_dn, st, nh):
                q = 2 * st + nh
                dve.wait_ge(dn_done, n_dn + q + 1)
                yp = y[:, st, nh * HALF:(nh + 1) * HALF]
                dve.tensor_tensor(yp, yp, psB[:, q % 4, :], ALU.add).then_inc(psb_drained, 1)

            dve.wait_ge(x1_scaled, ST)
            gated_unit(0, 0, 0)
            gated_unit(2, 0, 1)

            def group(it, j):
                gated_unit(8 * it + (4 + 4 * j), (j + 1) % 2, 0)
                for q in range(16):
                    add_down(32 * it + 16 * j, q // 2, q % 2)
                gated_unit(8 * it + (4 + 4 * j + 2), (j + 1) % 2, 1)

            with dve.Fori(0, PAIRED) as it:
                for j in range(2):
                    group(it, j)
            group(PAIRED, 0)
            for c in range(2):
                gated_unit(4 * (GROUPS - 1) + 2 * c, 0, c)
            n_dn = 16 * (GROUPS - 2)
            dve.wait_ge(ln_rows, 64)
            for st in range(ST + 1):
                if st < ST:
                    for nh in range(2):
                        add_down(n_dn, st, nh)
                        dve.wait_ge(psb_drained, X_Q + n_dn + 2 * st + nh + 1)
                        op = dve.bn_stats(stats[:, st % 2, nh, :], y[:, st, nh * HALF:(nh + 1) * HALF])
                    ln_chain(op)
                    dve.bn_aggr(mv[:, st % 2, :], stats[:, st % 2, :, :]).then_inc(ln_stats, 1)
                if st >= 1 and st - 1 in LN_AWAY:
                    b2 = (st - 1) % 2
                    dve.wait_ge(ln_std, ST + st)
                    ln_chain(dve.reciprocal(std[:, b2, 1:2], std[:, b2, 0:1]))
                    dve.scalar_tensor_tensor(out=shift[:, :], in0=mv[:, b2, 0:1], scalar=-1.0,
                                             in1=std[:, b2, 1:2], op0=ALU.mult, op1=ALU.mult)\
                       .then_inc(ln_shift, 1)
                elif st >= 1:
                    ln_finish(ST + st - 1, st - 1, 2 if st == ST else 1)

        @block.tensor
        def _(pe):
            def product(dst, w, v, first, last):
                pe.matmul(dst, w[0], v[0], start=first, stop=False)
                pe.matmul(dst, w[0], v[1], start=False, stop=False)
                return pe.matmul(dst, w[1], v[0], start=False, stop=last)

            def act_cols(k, cols):
                return act_hi[:, k, cols], act_lo[:, k, cols]

            def unit_w(slot):
                return [as_chunks(w[:, slot, :]) for w in (w_hi, w_lo)]

            def feature_major(dst, slot, n):
                w = unit_w(slot)
                for k in range(KC):
                    op = product(dst, (w[0][:, k, :], w[1][:, k, :]),
                                 act_cols(k, slice(n * HALF, (n + 1) * HALF)), k == 0, k == KC - 1)
                return op

            pe.wait_ge(consts_ready, 2)
            for Q in range(X_Q):
                st, h = divmod(Q, 2)
                k = Q - X_Q // 2
                if k == 0:
                    pe.wait_ge(q_lo, X_Q // 2)
                    pe.wait_ge(wlo_ready, 1)
                if k >= 0:
                    w = unit_w(0)
                    product(psA[:, 0, :], (w[0][:, k, :], w[1][:, k, :]), act_cols(k, slice(0, HALF)),
                            k == 0, k == KC - 1)
                if h == 0:
                    pe.wait_ge(x_loaded[st % 4], 16 * (st // 4 + 1))
                if Q >= 4:
                    pe.wait_ge(q_lo, Q - 3)
                for c in range(4 * h, 4 * h + 4):
                    op = pe.transpose(x_bank(Q)[:, (c % 4) * P:(c % 4 + 1) * P],
                                      x_tile[:, st % 4, c * P:(c + 1) * P], ident[:, :])
                op.then_inc(q_done, 2 if Q == X_Q - 1 else 1)

            pe.wait_ge(q_lo, X_Q)
            with pe.Fori(0, 3) as i:
                for c in range(4):
                    pe.wait_ge(wlo_ready, 6 * i + (c + 1))
                    for n in range(1 if c == 0 else 0, 2):
                        Q = 2 * c + n
                        pe.wait_ge(q_lo, 12 * i + (X_Q + Q - 3))
                        op = feature_major(psA[:, Q % 4, :], c % 3, n)
                        op.then_inc(q_done, 1)
                pe.wait_ge(wlo_ready, 6 * i + 6)
                for v in range(4):
                    pe.wait_ge(q_lo, 12 * i + (X_Q + 8 + v - 3))
                    for s2 in range(2):
                        st = 2 * v + s2
                        for k in range(KC):
                            slot = (4 + k // 4) % 3
                            w = [t[:, slot, (k % 4) * 256:(k % 4 + 1) * 256] for t in (w_hi, w_lo)]
                            op = product(psA[:, v, s2 * 256:(s2 + 1) * 256],
                                         act_cols(k, slice(st * P, (st + 1) * P)), w,
                                         k == 0, k == KC - 1)
                    op.then_inc(q_done, 1)
                pe.wait_ge(wlo_ready, 6 * i + 7)
                pe.wait_ge(q_lo, 12 * i + (X_Q + 9))
                feature_major(psA[:, 0, :], 0, 0).then_inc(q_done, 1)

            bank_free = {4: (conv_act, 1), 5: (conv_act, 2), 6: (conv_act, 3), 7: (conv_act, 4),
                         8: (conv_act, 5), 9: (conv_act, 6), 10: (conv_dve, 1), 11: (conv_dve, 2),
                         12: (gate_step, 1), 13: (gate_step, 2)}
            for c in range(7):
                u = PROJ_UNITS + c
                pe.wait_ge(wlo_ready, u + 1)
                for n in range(1 if c == 0 else 0, 2):
                    v = 2 * c + n
                    if v in bank_free:
                        pe.wait_ge(*bank_free[v])
                    if CONV_ORDER[c][0] != "f":
                        feature_major(psB[:, v % 4, :], u % 3, n).then_inc(conv_done, 1)
                        continue
                    for k in range(KC):
                        for part, x_t in enumerate(act_cols(k, slice(n * HALF, (n + 1) * HALF))):
                            op = pe.matmul(psB[:, v % 4, :], unit_w(u % 3)[0][:, k, :], x_t,
                                           start=k == 0 and part == 0, stop=k == KC - 1 and part == 1)
                    op.then_inc(conv_done, 1)

            def scores(s, a):
                pr, h, g = STEPS[s]
                par, W = pr % 2, width(s)
                if h == 0 and g == 0 and a == 0:
                    pe.wait_ge(qkv_loaded[par], 16 * 7 * (pr // 2 + 1))
                if s == 0 and a == 0:
                    pe.wait_ge(fixed_ready, 4)
                    pe.wait_ge(consts_ready, 8)
                    pe.wait_ge(q_lo, X_Q + 3 * KIND_Q)
                    pe.wait_ge(conv_act, 1)
                t, i = 2 * s + a, 2 * g + a
                if t >= 2:
                    if t - 2 < 32:
                        pe.wait_ge(z_read_act, t - 1)
                    else:
                        pe.wait_ge(z_read_dve, t - 2 - 32 + 1)
                q = q_st[par][h][:, i * P:(i + 1) * P]
                masked = kind(s) != DIL
                for b, c0 in enumerate(range(0, W, HALF)):
                    n = min(HALF, W - c0)
                    last = c0 + n == W
                    z = psA[:, 2 * a + b, 0:n]
                    pe.matmul(z, q, kh_st[par][h][:, c0:c0 + n], start=True, stop=False)
                    op = pe.matmul(z, q, kl_st[par][h][:, c0:c0 + n], start=False,
                                   stop=not (masked and last))
                    if masked and last:
                        op = pe.matmul(psA[:, 2 * a + b, n - 256:n], ident_bf[:, :],
                                       masks[:, int(kind(s) == SB), a, :], start=False, stop=True)
                op.then_inc(z_ready, 1)

            def transposes(s, j):
                k = CUM[s] + j
                if k >= 2:
                    pe.wait_ge(pt_lo_done, k - 1)
                else:
                    pe.wait_ge(conv_dve, 4)
                    pe.wait_ge(gate_step, 2)
                for a in range(2):
                    if j == 0:
                        if on_dve(s, a):
                            pe.wait_ge(probs_ready_dve, finished(s, a, True))
                        else:
                            pe.wait_ge(probs_ready, finished(s, a, False))
                    for b in range(2):
                        kb = 2 * j + b
                        unseen = a == 0 and kb == 2 * STEPS[s][2] + 1
                        op = pe.transpose(psB[:, k % 2, b * 256 + a * P:b * 256 + (a + 1) * P],
                                          zeros[:, :] if unseen else
                                          probs[s % 3][:, a, kb * P:(kb + 1) * P], ident[:, :])
                op.then_inc(pt_ready, 1)

            def values(s, j):
                pr, h, g = STEPS[s]
                k = CUM[s] + j
                if j == 0 and s >= 2:
                    pe.wait_ge(o_lo, s - 1)
                pe.wait_ge(pt_lo_done, k + 1)
                for b in range(2):
                    v = [v_t[pr % 2][:, part, 2 * j + b, h * HD:h * HD + P] for part in range(2)]
                    op = product(psB[:, 2 + s % 2, 0:256], v, (pt_hi[:, k % 3, b, :], pt_lo[:, k % 3, b, :]),
                                 j == 0 and b == 0, j == g and b == 1)
                op.then_inc(pv_done, 1)

            for s in range(2):
                for a in range(2):
                    scores(s, a)
            for k, (s, j) in enumerate(QUANTA):
                transposes(s, j)
                for r, a in TILES:
                    if start(r, a) == k:
                        scores(r, a)
                if k >= 2:
                    values(*QUANTA[k - 2])
            values(*QUANTA[-2])
            values(*QUANTA[-1])

            pe.wait_ge(conv_split, 2)
            pe.wait_ge(o_lo, NS)
            pe.wait_ge(z_read_dve, 64)

            def x1_transposes(st):
                pe.wait_ge(ln_done, st + 1)
                for h in range(2):
                    q = 2 * st + h
                    if q >= 4:
                        pe.wait_ge(psb_drained, q - 3)
                    for k in range(4):
                        c = 4 * h + k
                        op = pe.transpose(psB[:, q % 4, k * P:(k + 1) * P], y[:, st, c * P:(c + 1) * P],
                                          ident[:, :])
                    op.then_inc(x1_t, 1)

            for nh in range(2):
                for st in range(ST):
                    q = nh * ST + st
                    if q >= 4:
                        pe.wait_ge(y_added, q - 3)
                    for k in range(KC):
                        u = 4 * nh + k // 2
                        if st == 0 and k % 2 == 0:
                            pe.wait_ge(w3lo_ready, u + 1)
                        w = [t[:, (k % 2) * HALF:(k % 2 + 1) * HALF] for t in w3_unit(u)]
                        op = product(psA[:, q % 4, :], act_cols(k, slice(st * P, (st + 1) * P)), w,
                                     k == 0, k == KC - 1)
                    op.then_inc(wo_done, 1)
                    if nh == 1 and st >= 2:
                        x1_transposes(st - 2)

            def gated_part(slot, n, m, ks=range(KC)):
                w = [as_chunks(t[:, slot + m, :]) for t in (w3_hi, w3_lo)]
                for k in ks:
                    op = product(psA[:, 2 * n + m, :], (w[0][:, k, :], w[1][:, k, :]),
                                 act_cols(k, slice(n * HALF, (n + 1) * HALF)), k == 0, k == KC - 1)
                return op

            def gate_up(u, slot, n_gu, halves=range(2)):
                pe.wait_ge(w3lo_ready, u + 2)
                for n in halves:
                    if not (isinstance(n_gu, int) and n_gu == 0):
                        pe.wait_ge(h_done, n_gu + (n - 1))
                    gated_part(slot, n, 0)
                    gated_part(slot, n, 1).then_inc(gu_done, 1)

            def down(u, slot, n_dn, par, n_h):
                pe.wait_ge(w3lo_ready, u + 2)
                pe.wait_ge(hlo_done, n_h)
                for q in range(16):
                    st, nh = divmod(q, 2)
                    pe.wait_ge(psb_drained, n_dn + (X_Q + q - 3))
                    for ch in range(2):
                        w = [t[:, slot + ch, nh * HALF:(nh + 1) * HALF] for t in (w3_hi, w3_lo)]
                        cols = slice(st * P, (st + 1) * P)
                        op = product(psB[:, q % 4, :], (h_hi[:, par, ch, cols], h_lo[:, par, ch, cols]), w,
                                     ch == 0, ch == 1)
                    op.then_inc(dn_done, 1)

            pe.wait_ge(psb_drained, X_Q // 2)
            pe.wait_ge(y_added, 2 * ST)
            pe.wait_ge(w3lo_ready, 10)
            gated_part(2, 0, 0)
            x1_transposes(ST - 2)
            gated_part(2, 0, 1, range(0, 3))
            x1_transposes(ST - 1)
            gated_part(2, 0, 1, range(3, KC)).then_inc(gu_done, 1)
            pe.wait_ge(psb_drained, X_Q)
            gate_up(8, 2, 0, [1])
            gate_up(10, 4, 2)

            def group(it, j):
                at = 12 + 6 * j
                gate_up(12 * it + at, 0, 8 * it + (4 + 4 * j))
                down(12 * it + (at + 2), 2, 32 * it + 16 * j, j % 2, 8 * it + (4 + 4 * j))
                gate_up(12 * it + (at + 4), 4, 8 * it + (4 + 4 * j + 2))

            with pe.Fori(0, PAIRED) as it:
                for j in range(2):
                    group(it, j)
            group(PAIRED, 0)
            gate_up(66, 0, 4 * (GROUPS - 1))
            gate_up(68, 2, 4 * (GROUPS - 1) + 2)

            def last_down(q, ch):
                st, nh = divmod(q, 2)
                slot, par, c = (4, 5, 0, 1)[ch], 1 - ch // 2, ch % 2
                w = [t[:, slot, nh * HALF:(nh + 1) * HALF] for t in (w3_hi, w3_lo)]
                cols = slice(st * P, (st + 1) * P)
                return product(psB[:, q % 4, :], (h_hi[:, par, c, cols], h_lo[:, par, c, cols]), w,
                               ch == 0, ch == 3)

            n_dn = 16 * (GROUPS - 2)
            for q in range(16):
                pe.wait_ge(psb_drained, n_dn + (X_Q + q - 3))
                if q == 0:
                    pe.wait_ge(w3lo_ready, 73)
                    pe.wait_ge(hlo_done, 4 * GROUPS - 2)
                    for q2 in range(2):
                        if q2:
                            pe.wait_ge(psb_drained, n_dn + (X_Q + q2 - 3))
                        for ch in range(3):
                            last_down(q2, ch)
                    pe.wait_ge(w3lo_ready, 74)
                    pe.wait_ge(hlo_done, 4 * GROUPS)
                for ch in range(3 if q < 2 else 0, 4):
                    op = last_down(q, ch)
                op.then_inc(dn_done, 1)


_NAMES = ["x", "w_in", "f_bias", "conv_w", "w_out", "rel_bias", "ln1_g", "ln1_b", "w_gate", "w_up",
          "w_down", "ln2_g", "ln2_b"]


def kernel(**inputs):
    import numpy as _np
    import concourse.bacc as _bacc
    from concourse import mybir as _mybir
    from concourse.bass_utils import run_bass_kernel_spmd as _run

    nc = _bacc.Bacc("TRN2", target_bir_lowering=False, num_devices=1)
    arrays, args = {}, []
    for name in _NAMES:
        a = _np.ascontiguousarray(inputs[name])
        arrays[f"in_{name}"] = a
        args.append(nc.dram_tensor(f"in_{name}", a.shape, _mybir.dt.from_np(a.dtype),
                                   kind="ExternalInput").ap())
    args.append(nc.dram_tensor("out_x", (1, S, D), F32, kind="ExternalOutput").ap())
    layer(nc, *args)
    r = _run(nc, [arrays], core_ids=[0])
    return r.results[0]["out_x"]
```
